# Optimizing a Trainium2 kernel written in Bass

```python
import math
import jax
import jax.numpy as jnp
from jax import lax
import numpy as np

D_MODEL = 1024
BATCH = 1
SEQ = 512
DEPTH = 1

HEAD_DIM = 64
N_HEADS_SB = 8
N_HEADS_DIL = 8
D_SB = N_HEADS_SB * HEAD_DIM
D_DIL = N_HEADS_DIL * HEAD_DIM
D_MIX = D_SB + D_DIL
D_FF = 2816
DIL_CONFIGS = ((128, 1), (512, 4), (2048, 16))
BLOCK = 128
N_BUCKETS = 32
MAX_DISTANCE = 2048
N_MOD = 9
EPS = 1e-6
NEG_INF = -1e30

kernel_name = 'hybrid_stickbreak_dilated_macaron_adaln'

def rmsnorm(x, g):
    x32 = x.astype(jnp.float32)
    y = x32 * lax.rsqrt(jnp.mean(x32 * x32, axis=-1, keepdims=True) + EPS)
    return y.astype(x.dtype) * g

def modulate(x, g, shift, scale):
    return rmsnorm(x, g) * (1 + scale[:, None, :]) + shift[:, None, :]

def swiglu(h, w_gate, w_up, w_down):
    return (jax.nn.silu(h @ w_gate) * (h @ w_up)) @ w_down

def to_heads(a, n_heads):
    b, s, _ = a.shape
    return a.reshape(b, s, n_heads, HEAD_DIM).transpose(0, 2, 1, 3)

def from_heads(a):
    b, h, s, d = a.shape
    return a.transpose(0, 2, 1, 3).reshape(b, s, h * d)

def t5_causal_bucket(n):
    max_exact = N_BUCKETS // 2
    nf = np.maximum(n, 1).astype(np.float32)
    large = max_exact + (np.log(nf / max_exact) / math.log(MAX_DISTANCE / max_exact)
                         * (N_BUCKETS - max_exact)).astype(np.int32)
    large = np.minimum(large, N_BUCKETS - 1)
    return np.where(n < max_exact, n, large).astype(np.int32)

def stick_breaking_attention(q, k, v):
    b, h, s, dh = q.shape
    n_blk = s // BLOCK
    scale = dh ** -0.5
    key_pos = jnp.arange(s)

    def one_block(blk):
        qb = lax.dynamic_slice_in_dim(q, blk * BLOCK, BLOCK, axis=2)
        z = jnp.einsum('bhtd,bhsd->bhts', qb, k).astype(jnp.float32) * scale
        q_pos = blk * BLOCK + jnp.arange(BLOCK)
        causal = key_pos[None, :] < q_pos[:, None]
        log_not = jnp.where(causal, jax.nn.log_sigmoid(-z), 0.0)
        suffix = lax.cumsum(log_not, axis=3, reverse=True) - log_not
        w = jnp.where(causal, jnp.exp(jax.nn.log_sigmoid(z) + suffix), 0.0)
        return jnp.einsum('bhts,bhsd->bhtd', w.astype(v.dtype), v)

    out = lax.map(one_block, jnp.arange(n_blk))
    return out.transpose(1, 2, 0, 3, 4).reshape(b, h, s, dh)

def dilated_config(q, k, v, bias_table, window, dilation):
    b, h, s, dh = q.shape
    n_steps = window // dilation
    sub_len = s // dilation
    n_blk = -(-sub_len // BLOCK)
    pad = n_blk * BLOCK - sub_len

    def to_residue(a):
        a = a.reshape(b, h, sub_len, dilation, dh).transpose(0, 1, 3, 2, 4)
        a = jnp.pad(a, ((0, 0), (0, 0), (0, 0), (0, pad), (0, 0)))
        return a.reshape(b, h, dilation, n_blk, BLOCK, dh)

    def with_prev(a):
        prev = jnp.pad(a, ((0, 0), (0, 0), (0, 0), (1, 0), (0, 0), (0, 0)))[:, :, :, :-1]
        return jnp.concatenate([prev, a], axis=4)

    qr = to_residue(q)
    kb = with_prev(to_residue(k))
    vb = with_prev(to_residue(v))
    z = jnp.einsum('bhrnqd,bhrnkd->bhrnqk', qr, kb).astype(jnp.float32) * (dh ** -0.5)

    step = BLOCK + np.arange(BLOCK)[:, None] - np.arange(2 * BLOCK)[None, :]
    in_band = (step >= 0) & (step <= n_steps)
    has_prev = (np.arange(n_blk)[:, None, None] > 0) | (np.arange(2 * BLOCK)[None, None, :] >= BLOCK)
    valid = in_band[None] & has_prev

    bias = bias_table[t5_causal_bucket(np.arange(n_steps + 1) * dilation)]
    bias = bias[np.clip(step, 0, n_steps)].astype(jnp.float32)
    z = z + bias.transpose(2, 0, 1)[None, :, None, None]
    z = jnp.where(valid[None, None, None], z, NEG_INF)

    m = jnp.max(z, axis=-1, keepdims=True)
    e = jnp.exp(z - m)
    denom = jnp.sum(e, axis=-1)
    o = jnp.einsum('bhrnqk,bhrnkd->bhrnqd', e.astype(v.dtype), vb) / denom[..., None].astype(v.dtype)
    lse = m[..., 0] + jnp.log(denom)

    def from_residue(a):
        a = a.reshape(b, h, dilation, n_blk * BLOCK, a.shape[-1])[:, :, :, :sub_len]
        return a.transpose(0, 1, 3, 2, 4).reshape(b, h, s, a.shape[-1])

    return from_residue(o), from_residue(lse[..., None])[..., 0]

def dilated_attention(q, k, v, bias_table):
    outs, lses = [], []
    for window, dilation in DIL_CONFIGS:
        o, lse = dilated_config(q, k, v, bias_table, window, dilation)
        outs.append(o)
        lses.append(lse)
    alpha = jax.nn.softmax(jnp.stack(lses, axis=0), axis=0)
    return jnp.einsum('cbhs,cbhsd->bhsd', alpha.astype(q.dtype), jnp.stack(outs, axis=0))

def token_mixer(h, w_in, g_sb_out, g_dil_out, w_out, rel_bias):
    qkv = h @ w_in
    q_sb, k_sb, v_sb, q_dil, k_dil, v_dil = jnp.split(
        qkv, [D_SB, 2 * D_SB, 3 * D_SB, 3 * D_SB + D_DIL, 3 * D_SB + 2 * D_DIL], axis=-1)
    o_sb = stick_breaking_attention(to_heads(q_sb, N_HEADS_SB), to_heads(k_sb, N_HEADS_SB),
                                    to_heads(v_sb, N_HEADS_SB))
    o_dil = dilated_attention(to_heads(q_dil, N_HEADS_DIL), to_heads(k_dil, N_HEADS_DIL),
                              to_heads(v_dil, N_HEADS_DIL), rel_bias)
    o_sb = rmsnorm(o_sb, g_sb_out[:, None, :])
    o_dil = rmsnorm(o_dil, g_dil_out[:, None, :])
    o = jnp.concatenate([from_heads(o_sb), from_heads(o_dil)], axis=-1)
    return o @ w_out

def setup_inputs(seed: int = 0) -> dict:
    key = jax.random.key(seed)
    ks = jax.random.split(key, 20)
    f32 = jnp.float32

    def nrm(k, shape, scale):
        return jax.random.normal(k, shape, f32) * scale

    def gain(k, shape):
        return 1.0 + 0.05 * jax.random.normal(k, shape, f32)

    L, D = DEPTH, D_MODEL
    return {
        'x': nrm(ks[0], (BATCH, SEQ, D), 1.0),
        'c': nrm(ks[1], (BATCH, D), 1.0),
        'w_ada': nrm(ks[2], (L, D, N_MOD * D), 0.5 * D ** -0.5),
        'b_ada': nrm(ks[3], (L, N_MOD * D), 0.02),
        'g_ffn1': gain(ks[4], (L, D)),
        'w1_gate': nrm(ks[5], (L, D, D_FF), D ** -0.5),
        'w1_up': nrm(ks[6], (L, D, D_FF), D ** -0.5),
        'w1_down': nrm(ks[7], (L, D_FF, D), D_FF ** -0.5),
        'g_mix': gain(ks[8], (L, D)),
        'w_in': nrm(ks[9], (L, D, 3 * D_MIX), D ** -0.5),
        'g_sb_out': gain(ks[10], (L, N_HEADS_SB, HEAD_DIM)),
        'g_dil_out': gain(ks[11], (L, N_HEADS_DIL, HEAD_DIM)),
        'w_out': nrm(ks[12], (L, D_MIX, D), D_MIX ** -0.5),
        'rel_bias': nrm(ks[13], (N_BUCKETS, N_HEADS_DIL), 0.5),
        'g_ffn2': gain(ks[14], (L, D)),
        'w2_gate': nrm(ks[15], (L, D, D_FF), D ** -0.5),
        'w2_up': nrm(ks[16], (L, D, D_FF), D ** -0.5),
        'w2_down': nrm(ks[17], (L, D_FF, D), D_FF ** -0.5),
        'g_final': gain(ks[18], (D,)),
    }

def reference(x, c, w_ada, b_ada, g_ffn1, w1_gate, w1_up, w1_down, g_mix, w_in, g_sb_out,
              g_dil_out, w_out, rel_bias, g_ffn2, w2_gate, w2_up, w2_down, g_final):
    for l in range(DEPTH):
        mod = (jax.nn.silu(c) @ w_ada[l] + b_ada[l]).reshape(c.shape[0], N_MOD, D_MODEL)
        sh1, sc1, gt1, sh2, sc2, gt2, sh3, sc3, gt3 = [mod[:, i] for i in range(N_MOD)]
        h = modulate(x, g_ffn1[l], sh1, sc1)
        x = x + 0.5 * gt1[:, None, :] * swiglu(h, w1_gate[l], w1_up[l], w1_down[l])
        h = modulate(x, g_mix[l], sh2, sc2)
        x = x + gt2[:, None, :] * token_mixer(h, w_in[l], g_sb_out[l], g_dil_out[l], w_out[l], rel_bias)
        h = modulate(x, g_ffn2[l], sh3, sc3)
        x = x + 0.5 * gt3[:, None, :] * swiglu(h, w2_gate[l], w2_up[l], w2_down[l])
    return rmsnorm(x, g_final)


_drawn_inputs = setup_inputs


def setup_inputs(seed=0):
    import zlib

    import numpy as np

    out = dict(_drawn_inputs(seed))
    spreads = {}
    factors = {'g_ffn1': 7.683, 'g_mix': 3.881, 'g_sb_out': 26.643, 'g_dil_out': 26.973, 'g_ffn2': 7.951}
    for name, (base, spread) in spreads.items():
        noise = np.random.default_rng([zlib.crc32(name.encode()), seed]).standard_normal(out[name].shape)
        drawn = base * np.exp(spread * noise) if base else spread * noise
        out[name] = jnp.asarray(drawn.astype(out[name].dtype))
    for name, factor in factors.items():
        out[name] = (out[name] * factor).astype(out[name].dtype)
    return out
```

```python
import numpy as np
import concourse.bass as bass
from concourse import mybir
from contextlib import ExitStack

SEQ, D, D_FF, DH = 512, 1024, 2816, 64
P = 128
KC = D // P
FC = D_FF // P
NB = SEQ // P
PAIRS = 8
N_SB = 4
D_GRP = 512
EPS = 1e-6
NEG = -1e30
PACK = sum(SEQ - P * j for j in range(NB))
ROW = 640
ADA_FIRST, ADA_COLS = 8, 256
ADA_BLOCKS = 9 * D // ADA_COLS
ARENA = 2 * FC * SEQ
SLOT = 2048


def build(nc, x, c, w_ada, b_ada, g_ffn1, w1_gate, w1_up, w1_down, g_mix, w_in, g_sb_out, g_dil_out, w_out,
          rel_bias, g_ffn2, w2_gate, w2_up, w2_down, g_final, masks, onehot, bias_rows, bias_copies, out):
    f32, f32r, i32 = mybir.dt.float32, mybir.dt.float32r, mybir.dt.int32
    ALU = mybir.AluOpType
    ACT = mybir.ActivationFunctionType
    ds = bass.ds
    ctx = ExitStack()
    with ctx:
        def sb(name, shape, dt=f32):
            return ctx.enter_context(nc.sbuf_tensor(name, shape, dt))

        def sem(name):
            return ctx.enter_context(nc.semaphore(name))

        xT = sb("xT", [P, KC * SEQ])
        hh = sb("hh", [P, KC, SEQ], f32r)
        hl = sb("hl", [P, KC, SEQ], f32r)
        w_raw = sb("w_raw", [P, 2 * SLOT])
        w_hi = sb("w_hi", [P, 2 * SLOT], f32r)
        w_lo = sb("w_lo", [P, 2 * SLOT], f32r)
        ada = sb("ada", [P, 8, ADA_COLS])
        tmp = sb("tmp", [P, 5, SEQ])
        ident = sb("ident", [P, P])
        halves = sb("halves", [P, P])
        ones = sb("ones", [P, P])
        maskr = sb("maskr", [P, 4, P], f32r)
        vecs = sb("vecs", [P, 120])
        mod = sb("mod", [P, 72])
        amp = sb("amp", [P, 3 * KC])
        hgate = sb("hgate", [P, 3 * KC])
        csil = sb("csil", [P, KC])
        eps = sb("eps", [P, 2])
        stats = sb("stats", [P, 2, 4, NB])
        rel = sb("rel", [33, 8])
        carrier = sb("carrier", [P, 1])

        arena_at = (nc.sbuf_base + 31) // 32 * 32
        sb("arena", [P, ARENA])
        at = [0]

        def place(name, shape, dt=f32):
            size = 4 * int(np.prod(shape[1:]))
            assert at[0] + size <= 4 * ARENA
            at[0] += size
            return nc.alloc_sbuf_tensor_at(name, shape, dt, offset=arena_at + at[0] - size)

        x_nat = place("x_nat", [P, NB, D])
        ada0 = [place(f"ada0_{b}", [P, 8, ADA_COLS]) for b in range(ADA_FIRST)]
        rows = place("rows", [P, P])
        maskf = place("maskf", [P, 5, P])
        oneh = place("oneh", [P, ROW])
        brow = place("brow", [P, ROW])
        at[0] = 0
        guh = place("guh", [P, FC * SEQ], f32r)
        gul = place("gul", [P, FC * SEQ], f32r)
        at[0] = 0
        oTh = place("oTh", [P, PAIRS * SEQ], f32r)
        oTl = place("oTl", [P, PAIRS * SEQ], f32r)
        qh, ql = place("qh", [P, SEQ], f32r), place("ql", [P, SEQ], f32r)
        kh, kl = place("kh", [P, SEQ], f32r), place("kl", [P, SEQ], f32r)
        vsb = place("vsb", [P, SEQ])
        vph = place("vph", [P, NB, 3, DH], f32r)
        vpl = place("vpl", [P, NB, 3, DH], f32r)
        E = [place("E0", [P, PACK]), place("E1", [P, PACK])]
        sph, spl = place("sph", [P, PACK], f32r), place("spl", [P, PACK], f32r)
        wth, wtl = place("wth", [P, PACK], f32r), place("wtl", [P, PACK], f32r)
        at[0] = 0
        o_nat = place("o_nat", [P, NB, D])

        sil = [tmp[:, 0, :], tmp[:, 1, :]]
        gut = [tmp[:, 2, :], tmp[:, 3, :]]
        ssum = tmp[:, 4, :]
        adaf = ada[:, :, :].rearrange("p t n -> p (t n)")
        tbl = [adaf[:, SEQ * n:SEQ * n + SEQ] for n in range(2)]
        ident_r, ntri, nones, negm = (maskr[:, n, :] for n in range(4))

        ps = ctx.enter_context(nc.psum_tensor("ps", [P, 8, SEQ], f32))

        def bank(n):
            return ps[:, n, :]

        B_Y, B_MOD, B_ST = (4, 5), 6, 7
        B_Z, B_O, B_P = (0, 3), 6, 7

        def two(ap, b0):
            return [(ap[:, 0:512], bank(b0)),
                    (ap[:, 512:1280].rearrange("p (b n) -> p b n", b=2), ps[:, b0 + 1:b0 + 3, 0:384])]

        OFF = [0, 512, 896, 1152]
        PB = [(0, 0), (1, 0), (2, 0), (2, 256)]
        WID = [SEQ - P * j for j in range(NB)]
        by_token = bank(B_P).rearrange("p (b e n) -> p b e n", b=NB, e=2)

        s_vec, s_masks, s_x, s_oneh, s_rel1, s_ones = (sem(n) for n in ("s_vec", "s_masks", "s_x", "s_oneh", "s_rel1", "s_ones"))
        s_maskr, s_vect, s_vecs, s_csil, s_eps = (sem(n) for n in ("s_maskr", "s_vect", "s_vecs", "s_csil", "s_eps"))
        s_xt, s_xev, s_brow, s_browc, s_browd = (sem(n) for n in ("s_xt", "s_xev", "s_brow", "s_browc", "s_browd"))
        s_ada0 = [sem(f"s_ada0_{n}") for n in range(ADA_FIRST)]
        s_sump, s_sumv, s_mod0, s_modv0, s_amp = (sem(n) for n in ("s_sump", "s_sumv", "s_mod0", "s_modv0", "s_amp"))
        s_adal, s_adac, s_adap, s_adam, s_modv = (sem(n) for n in ("s_adal", "s_adac", "s_adap", "s_adam", "s_modv"))
        s_adav = sem("s_adav")
        slots = {}
        for name, o, n in (("A", 0, SLOT), ("B", SLOT, SLOT), ("q", 0, 1024), ("k", 1024, 1024), ("v", 2048, 1024)):
            slots[name] = dict(raw=w_raw[:, o:o + n], hi=w_hi[:, o:o + n], lo=w_lo[:, o:o + n],
                               loaded=sem(f"s_loaded_{name}"), his=sem(f"s_hi_{name}"),
                               split=sem(f"s_split_{name}"))
        s_sq, s_ssum, s_stat, s_ln, s_rstd = (sem(n) for n in ("s_sq", "s_ssum", "s_stat", "s_ln", "s_rstd"))
        s_t, s_h, s_hh, s_hl = (sem(n) for n in ("s_t", "s_h", "s_hh", "s_hl"))
        s_gate, s_sil, s_up, s_gu, s_guh, s_gul = (sem(n) for n in ("s_gate", "s_sil", "s_up", "s_gu", "s_guh", "s_gul"))
        s_half, s_y, s_xn = sem("s_half"), sem("s_y"), sem("s_xn")
        s_pq, s_qh, s_qr, s_pk, s_kh, s_kr = (sem(n) for n in ("s_pq", "s_qh", "s_qr", "s_pk", "s_kh", "s_kr"))
        s_pv, s_vsb, s_vt, s_vh, s_vr, s_vz = (sem(n) for n in ("s_pv", "s_vsb", "s_vt", "s_vh", "s_vr", "s_vz"))
        s_s, s_abs, s_e, s_l, s_sp, s_sph, s_spl = (sem(n) for n in ("s_s", "s_abs", "s_e", "s_l", "s_sp", "s_sph", "s_spl"))
        s_tr, s_w, s_wh, s_wlo = (sem(n) for n in ("s_tr", "s_w", "s_wh", "s_wlo"))
        s_avh = sem("s_avh")
        s_tbl = [sem("s_tbl0"), sem("s_tbl1")]
        s_zt, s_nm, s_ex, s_rd, s_pn = (sem(n) for n in ("s_zt", "s_nm", "s_ex", "s_rd", "s_pn"))
        s_osq, s_ost, s_oln, s_ors, s_ot, s_oh, s_ol = (
            sem(n) for n in ("s_osq", "s_ost", "s_oln", "s_ors", "s_ot", "s_oh", "s_ol"))
        s_copies = sem("s_copies")
        s_fy, s_ft, s_fo, s_out = sem("s_fy"), sem("s_ft"), sem("s_fo"), sem("s_out")

        N_FFN1, N_DOWN1, N_OUT, N_FFN2, N_DOWN2 = 0, 11, 19, 21, 32
        GB, DB = FC // 2, KC
        ADA_LOOP = 2 * GB
        ADA_OUT = ADA_BLOCKS - ADA_FIRST - ADA_LOOP
        H0 = 2 * N_SB
        Y_OUT, Y_FFN2 = KC, 2 * KC

        def X(ch):
            return xT[:, SEQ * ch:SEQ * ch + SEQ]

        def part(t, n):
            return t[:, OFF[n]:OFF[n] + WID[n]]

        block = ctx.enter_context(nc.Block())

        @block.sync
        def _(sp):
            wv = w_ada[0].rearrange("(t p) n -> p t n", p=P)
            for b in range(ADA_FIRST):
                sp.dma_start(ada0[b][:], wv[:, :, b * ADA_COLS:(b + 1) * ADA_COLS]).then_inc(s_ada0[b], 16)

            def load(name, n, src):
                s = slots[name]
                sp.wait_ge(s["split"], n + 1)
                t, cols = src.shape[1], src.shape[2]
                dst = s["raw"][:, 0:t * cols].rearrange("p (t n) -> p t n", t=t)
                sp.dma_start(dst, src).then_inc(s["loaded"], 16)

            def load_ffn(wg, wu, wd, n0, n1):
                g = wg[0].rearrange("(t p) n -> p t n", p=P)
                u = wu[0].rearrange("(t p) n -> p t n", p=P)
                d = wd[0].rearrange("(t p) n -> p t n", p=P)
                with sp.Fori(0, GB) as i:
                    load("A", n0 + i, g[:, :, ds(i * 256, 256)])
                    load("B", n0 + i, u[:, :, ds(i * 256, 256)])
                with sp.Fori(0, DB) as m:
                    load("A", n1 + m, d[:, 0:11, ds(m * P, P)])
                    load("B", n1 + m, d[:, 11:22, ds(m * P, P)])

            load_ffn(w1_gate, w1_up, w1_down, N_FFN1, N_DOWN1)
            sp.wait_ge(s_browd, 16)
            sp.dma_start(bias_copies, bias_rows.unsqueeze(1).broadcast_to([8, P, ROW])).then_inc(s_copies, 16)
            wi = w_in[0].rearrange("(t p) n -> p t n", p=P)
            sp.wait_ge(slots["A"]["split"], N_OUT + 1)
            sp.wait_ge(slots["B"]["split"], N_OUT + 1)
            with sp.Fori(0, N_SB) as p:
                for j, name in enumerate("qkv"):
                    load(name, p, wi[:, :, ds(p * P + j * D_GRP, P)])

            def load_table(h):
                src = bass.AP(tensor=bias_copies.tensor, offset=(h - H0) * P * ROW + P - 1, ap=[[ROW - 1, P], [1, SEQ]])
                sp.dma_start(tbl[h % 2], src).then_inc(s_tbl[h % 2], 16)

            sp.wait_ge(s_copies, 16)
            sp.wait_ge(s_adam, ADA_LOOP + 1)
            load_table(H0)
            load_table(H0 + 1)
            for p in range(N_SB, PAIRS):
                for j, name in enumerate("qkv"):
                    lo_col = (p - N_SB) * P + (j + 3) * D_GRP
                    load(name, p, wi[:, :, lo_col:lo_col + P])
                if p > N_SB:
                    for h in (2 * p, 2 * p + 1):
                        sp.wait_ge(s_nm, h - H0 - 1)
                        load_table(h)
            for name in "qkv":
                sp.wait_ge(slots[name]["split"], PAIRS + 1)
            wo = w_out[0].rearrange("(t p) n -> p t n", p=P)
            with sp.Fori(0, 2) as i:
                load("A", N_OUT + i, wo[:, :, ds(i * 512, 256)])
                load("B", N_OUT + i, wo[:, :, ds(i * 512 + 256, 256)])
            load_ffn(w2_gate, w2_up, w2_down, N_FFN2, N_DOWN2)
            ov = out[0].rearrange("(b p) d -> p b d", p=P)
            for n in range(4):
                sp.wait_ge(s_fo, 2 * n + 2)
                sp.dma_start(ov[:, :, 256 * n:256 * n + 256], o_nat[:, :, 256 * n:256 * n + 256]).then_inc(s_out, 16)
            sp.wait_ge(s_out, 64)

        def ada_sums(tt, wait_ge, a, chain, base, done):
            cs = csil[:, :].unsqueeze(2).broadcast_to([P, KC, ADA_COLS])
            tt(a[:, :, :], a[:, :, :], cs, ALU.mult).then_inc(chain, 1)
            wait_ge(chain, base + 1)
            tt(a[:, 0:4, :], a[:, 0:4, :], a[:, 4:8, :], ALU.add).then_inc(chain, 1)
            wait_ge(chain, base + 2)
            tt(a[:, 0:2, :], a[:, 0:2, :], a[:, 2:4, :], ALU.add).then_inc(chain, 1)
            wait_ge(chain, base + 3)
            tt(a[:, 0, :], a[:, 0, :], a[:, 1, :], ALU.add).then_inc(done, 1)

        ADA_POOL, ADA_DVE = (1, 4, 6), (0, 2, 3, 5, 7)

        @block.gpsimd
        def _(pool):
            nc.gpsimd.memset(rel[:], 1.0).then_inc(s_rel1, 1)
            nc.gpsimd.memset(ones[:], 1.0).then_inc(s_ones, 1)
            nc.gpsimd.memset(eps[:, 0:1], EPS).then_inc(s_eps, 1)
            nc.gpsimd.memset(eps[:, 1:2], 1.0).then_inc(s_eps, 1)
            pool.wait_ge(s_csil, 1)
            for n, b in enumerate(ADA_POOL):
                pool.wait_ge(s_ada0[b], 16)
                ada_sums(nc.gpsimd.tensor_tensor, pool.wait_ge, ada0[b], s_adac, 3 * n, s_sump)
            wv = w_ada[0].rearrange("(t p) n -> p t n", p=P)

            def ada_block(n):
                pool.wait_ge(s_adam, n + 1)
                pool.dma_start(ada[:], wv[:, :, ds((n + ADA_FIRST) * ADA_COLS, ADA_COLS)]).then_inc(s_adal, 16)
                pool.wait_ge(s_adal, 16 * n + 16)
                ada_sums(nc.gpsimd.tensor_tensor, pool.wait_ge, ada, s_adac, 3 * len(ADA_POOL) + 3 * n, s_adap)

            with pool.Fori(0, ADA_LOOP) as n:
                ada_block(n)
            pool.wait_ge(s_hl, 2 * KC)
            nc.gpsimd.memset(vph[:].bitcast(f32), 0.0).then_inc(s_vz, 1)
            nc.gpsimd.memset(vpl[:].bitcast(f32), 0.0).then_inc(s_vz, 1)
            with pool.Fori(0, N_SB) as p:
                for r in range(2):
                    h = 2 * p + r
                    pool.wait_ge(s_sp, h + 1)
                    pool.wait_ge(s_tr, h + 1)
                    nc.gpsimd.tensor_tensor(sph[:], E[r][:], ones[:, 0:1].broadcast_to([P, PACK]), ALU.mult).then_inc(s_sph, 1)
                    pool.wait_ge(s_sph, h + 1)
                    nc.gpsimd.tensor_tensor(spl[:], E[r][:], sph[:].bitcast(f32), ALU.subtract).then_inc(s_spl, 1)
            pool.wait_ge(s_nm, 2 * PAIRS - H0)
            with pool.Fori(ADA_LOOP, ADA_LOOP + ADA_OUT) as n:
                ada_block(n)

        @block.scalar
        def _(act):
            fn = nc.scalar.activation

            def hi(name, n):
                s = slots[name]
                act.wait_ge(s["loaded"], 16 * n + 16)
                fn(s["hi"], s["raw"], ACT.Copy).then_inc(s["his"], 1)

            parts = [(b_ada[0].rearrange("(r n) -> r n", n=P), 0, 72), (c[0].rearrange("(r n) -> r n", n=P), 72, 8),
                     (g_ffn1[0].rearrange("(r n) -> r n", n=P), 80, 8), (g_mix[0].rearrange("(r n) -> r n", n=P), 88, 8),
                     (g_ffn2[0].rearrange("(r n) -> r n", n=P), 96, 8), (g_final.rearrange("(r n) -> r n", n=P), 104, 8),
                     (g_sb_out[0].rearrange("(a b) n -> a (b n)", b=2), 112, 4),
                     (g_dil_out[0].rearrange("(a b) n -> a (b n)", b=2), 116, 4)]
            for src, o, n in parts:
                act.dma_start(rows[o:o + n, :], src).then_inc(s_vec, 16)
            act.dma_start(maskf[:], masks.rearrange("m p n -> p m n")).then_inc(s_masks, 16)
            act.dma_start(x_nat[:], x[0].rearrange("(b p) d -> p b d", p=P)).then_inc(s_x, 16)
            act.dma_start(oneh[0:33, :], onehot).then_inc(s_oneh, 16)
            act.wait_ge(s_rel1, 1)
            act.dma_start(rel[0:32, :], rel_bias).then_inc(s_oneh, 16)
            act.sem_inc(s_sil, 2)
            act.sem_inc(s_oln, 1)
            act.wait_ge(s_masks, 16)
            fn(ident[:], maskf[:, 0, :], ACT.Copy).then_inc(s_maskr, 1)
            fn(halves[:], maskf[:, 4, :], ACT.Copy).then_inc(s_maskr, 1)
            fn(maskr[:], maskf[:, 0:4, :], ACT.Copy).then_inc(s_maskr, 1)
            act.wait_ge(s_eps, 2)
            act.wait_ge(s_vecs, 1)
            fn(csil[:], vecs[:, 72:80], ACT.Silu).then_inc(s_csil, 1)
            for ch in range(KC):
                act.wait_ge(s_xt, ch + 1)
                fn(X(ch), bank(ch % 2), ACT.Copy).then_inc(s_xev, 1)
            act.wait_ge(s_brow, 1)
            fn(brow[0:8, 0:512], ps[0:8, 2, :], ACT.Copy).then_inc(s_browc, 1)
            fn(brow[0:8, 512:640], ps[0:8, 3, 0:128], ACT.Copy).then_inc(s_browc, 1)
            act.wait_ge(s_browc, 2)
            act.dma_start(bias_rows, brow[0:8, :]).then_inc(s_browd, 16)
            for ch in range(KC):
                act.wait_ge(s_xev, ch + 1)
                if ch >= 2:
                    act.wait_ge(s_ssum, ch)
                fn(gut[ch % 2], X(ch), ACT.Square).then_inc(s_sq, 1)

            def rstd(k):
                nc.scalar.preload_act_table_set("natural_log_exp_and_others")
                act.wait_ge(s_stat, k + 1)
                fn(ssum, bank(B_ST), ACT.Ln, bias=eps[:, 0:1], scale=1.0 / D).then_inc(s_ln, 1)
                act.wait_ge(s_ln, k + 1)
                fn(ssum, ssum, ACT.Exp, scale=-0.5).then_inc(s_rstd, 1)

            def modulated(k):
                rstd(k)
                for ch in range(KC):
                    act.wait_ge(s_h, KC * k + ch + 1)
                    fn(hh[:, ch, :], sil[ch % 2], ACT.Copy).then_inc(s_hh, 1)

            def square(k, ch, buf):
                act.wait_ge(s_xn, KC * (k - 1) + ch + 3)
                act.wait_ge(s_ssum, 9 * k + ch)
                fn(gut[buf], xT[:, ds(ch * SEQ, SEQ)], ACT.Square).then_inc(s_sq, 1)

            def ffn(f, n0, n1):
                modulated(2 * f)
                nc.scalar.preload_act_table_set("silu_and_others")
                with act.Fori(0, GB) as i:
                    j0 = 2 * i + FC * f
                    hi("B", n0 + i)
                    for r in range(2):
                        act.wait_ge(s_gate, j0 + r + 1)
                        act.wait_ge(s_gu, j0 + r + 1)
                        fn(sil[r], bank(r), ACT.Silu).then_inc(s_sil, 1)
                    hi("A", n0 + i + 1)
                    for r in range(2):
                        act.wait_ge(s_gu, j0 + r + 3)
                        fn(guh[:, ds(i * 1024 + SEQ * r, SEQ)], gut[r], ACT.Copy).then_inc(s_guh, 1)

                def down(m, r, last):
                    hi("B", n1 + m)
                    if not last:
                        act.wait_ge(s_half, KC * f + m + 1)
                        hi("A", n1 + m + 1)
                    square(2 * f + 1, m, r)

                with act.Fori(0, 3) as i:
                    for r in range(2):
                        down(2 * i + r, r, False)
                down(6, 0, False)
                down(7, 1, True)

            hi("A", N_FFN1)
            ffn(0, N_FFN1, N_DOWN1)

            def evac_q(p):
                act.wait_ge(s_pq, p + 1)
                fn(qh[:], bank(B_P), ACT.Copy, scale=DH ** -0.5).then_inc(s_qh, 1)

            def evac_k(p):
                act.wait_ge(s_pk, p + 1)
                fn(kh[:], bank(B_P), ACT.Copy).then_inc(s_kh, 1)

            def evac_v(p):
                act.wait_ge(s_pv, p + 1)
                fn(vsb[:], bank(B_P), ACT.Copy).then_inc(s_vsb, 1)
                act.wait_ge(s_vt, p + 1)
                fn(vph[:, :, 0:3:2, :], by_token, ACT.Copy).then_inc(s_vh, 1)

            def stick_softplus(h, r):
                act.wait_ge(s_abs, h + 1)
                fn(E[r][:], E[r][:], ACT.Exp, scale=-1.0).then_inc(s_e, 1)
                act.wait_ge(s_e, h + 1)
                fn(E[r][:], E[r][:], ACT.Ln, bias=eps[:, 1:2]).then_inc(s_l, 1)

            def stick_weights(h, r):
                act.wait_ge(s_tr, h + 2)
                for o, z in two(E[r], B_Z[r]):
                    last = fn(o, z, ACT.Exp)
                last.then_inc(s_w, 1)
                act.wait_ge(s_w, h + 1)
                act.wait_ge(s_avh, h + 1)
                fn(wth[:], E[r][:], ACT.Copy).then_inc(s_wh, 1)

            def dil_exp(h, r):
                act.wait_ge(s_nm, h - H0 + 1)
                for n in range(NB):
                    last = fn(part(E[r], n), part(E[r], n), ACT.Exp, bias=stats[:, r, 1, n:n + 1],
                              accum_out=stats[:, r, 2, n:n + 1])
                last.then_inc(s_ex, 1)

            def dil_weights(h, r):
                act.wait_ge(s_tr, h + 2)
                act.wait_ge(s_avh, h + 1)
                for o, z in two(wth, B_Z[r]):
                    last = fn(o, z, ACT.Copy)
                last.then_inc(s_wh, 1)

            def head_out(p):
                act.wait_ge(s_avh, 2 * p + 3)
                fn(gut[0], bank(B_O), ACT.Square).then_inc(s_osq, 1)
                act.wait_ge(s_ost, p + 1)
                fn(sil[1], bank(B_P), ACT.Ln, bias=eps[:, 0:1], scale=1.0 / DH).then_inc(s_oln, 1)
                act.wait_ge(s_oln, p + 2)
                fn(sil[1], sil[1], ACT.Exp, scale=-0.5).then_inc(s_ors, 1)
                act.wait_ge(s_ot, p + 2)
                fn(oTh[:, ds(p * SEQ, SEQ)], sil[0], ACT.Copy).then_inc(s_oh, 1)

            def mix_pair(p, dil, proj):
                h = 2 * p
                first, second = (dil_exp, dil_weights) if dil else (stick_softplus, stick_weights)
                if proj:
                    hi("q", p + 1)
                first(h, 0)
                if proj:
                    hi("k", p + 1)
                first(h + 1, 1)
                if proj:
                    evac_q(p + 1)
                    hi("v", p + 1)
                second(h, 0)
                if proj:
                    evac_k(p + 1)
                second(h + 1, 1)
                if proj:
                    evac_v(p + 1)
                head_out(p)

            nc.scalar.preload_act_table_set("natural_log_exp_and_others")
            for name in "qkv":
                act.wait_ge(s_half, KC)
                hi(name, 0)
            modulated(1)
            evac_q(0)
            evac_k(0)
            act.wait_ge(s_vz, 2)
            evac_v(0)
            with act.Fori(0, N_SB) as p:
                mix_pair(p, False, True)
            with act.Fori(N_SB, PAIRS - 1) as p:
                mix_pair(p, True, True)
            mix_pair(PAIRS - 1, True, False)

            hi("A", N_OUT)
            with act.Fori(0, 2) as i:
                hi("B", N_OUT + i)
                for r in range(4):
                    square(2, 4 * i + r, r % 2)
                    if r == 1:
                        hi("A", N_OUT + i + 1)
            ffn(1, N_FFN2, N_DOWN2)

            rstd(3)
            for ch in range(KC):
                act.wait_ge(s_ft, ch + 1)
                fn(o_nat[:, :, P * ch:P * ch + P], bank(ch % 2).rearrange("p (b n) -> p b n", b=NB),
                   ACT.Copy).then_inc(s_fo, 1)

        @block.vector
        def _(dve):
            tt, stt = nc.vector.tensor_tensor, nc.vector.scalar_tensor_tensor

            def lo(name, n):
                s = slots[name]
                dve.wait_ge(s["his"], n + 1)
                tt(s["lo"], s["raw"], s["hi"].bitcast(f32), ALU.subtract).then_inc(s["split"], 1)

            for s in slots.values():
                dve.sem_inc(s["split"], 1)
            dve.sem_inc(s_xn, 2)
            dve.sem_inc(s_gu, 2)
            dve.sem_inc(s_wlo, 2)
            dve.sem_inc(s_ot, 1)
            dve.sem_inc(s_modv, 1)
            nc.vector.memset(ssum, 0.0).then_inc(s_ssum, 1)
            dve.wait_ge(s_vect, 1)
            nc.vector.tensor_copy(vecs[:], ps[:, 4, 0:120]).then_inc(s_vecs, 1)
            dve.wait_ge(s_csil, 1)

            def add_squares(k, ch, buf):
                dve.wait_ge(s_sq, KC * k + ch + 1)
                dve.wait_ge(s_ssum, 9 * k + ch + 1)
                tt(ssum, ssum, gut[buf], ALU.add).then_inc(s_ssum, 1)

            for n, b in enumerate(ADA_DVE):
                dve.wait_ge(s_ada0[b], 16)
                ada_sums(tt, dve.wait_ge, ada0[b], s_adav, 3 * n, s_sumv)
                if n == 3:
                    for ch in range(KC):
                        add_squares(0, ch, ch % 2)
            lo("A", N_FFN1)
            dve.wait_ge(s_mod0, 1)
            tt(mod[:, 0:2 * ADA_FIRST], ps[:, B_MOD, 0:2 * ADA_FIRST], vecs[:, 0:2 * ADA_FIRST], ALU.add).then_inc(s_modv0, 1)
            dve.wait_ge(s_modv0, 1)

            def ada_vec(n, col):
                dve.wait_ge(s_adam, n + 2)
                o = 2 * ADA_FIRST + 2 * n
                tt(mod[:, ds(o, 2)], ps[:, B_MOD, col:col + 2], vecs[:, ds(o, 2)], ALU.add).then_inc(s_modv, 1)

            def amplitude(k, count):
                stt(amp[:, KC * k:KC * k + KC], mod[:, 24 * k + 8:24 * k + 16], 1.0, vecs[:, 80 + 8 * k:88 + 8 * k],
                    ALU.add, ALU.mult).then_inc(s_amp, 1)
                dve.wait_ge(s_amp, count)

            def gate_of(k, factor, count):
                nc.vector.tensor_scalar(hgate[:, KC * k:KC * k + KC], mod[:, 24 * k + 16:24 * k + 24], factor, None,
                                        ALU.mult).then_inc(s_amp, 1)
                dve.wait_ge(s_amp, count)

            def modulated(k):
                dve.wait_ge(s_rstd, k + 1)

                def h_lo(ch):
                    dve.wait_ge(s_hh, KC * k + ch + 1)
                    tt(hl[:, ch, :], sil[ch % 2], hh[:, ch, :].bitcast(f32), ALU.subtract).then_inc(s_hl, 1)

                for ch in range(KC):
                    tt(gut[ch % 2], X(ch), ssum, ALU.mult).then_inc(s_t, 1)
                    dve.wait_ge(s_t, KC * k + ch + 1)
                    nc.vector.tensor_scalar(sil[ch % 2], gut[ch % 2], amp[:, KC * k + ch:KC * k + ch + 1],
                                            mod[:, 24 * k + ch:24 * k + ch + 1], ALU.mult, ALU.add).then_inc(s_h, 1)
                    if ch >= 1:
                        h_lo(ch - 1)
                h_lo(KC - 1)
                nc.vector.memset(ssum, 0.0).then_inc(s_ssum, 1)

            def residual(y, ch, b, k, g):
                dve.wait_ge(s_y, y + 1)
                xs = xT[:, ds(ch * SEQ, SEQ)]
                stt(xs, bank(b), hgate[:, ds(ch + KC * g, 1)], xs, ALU.mult, ALU.add).then_inc(s_xn, 1)
                add_squares(k, ch, b % 2)

            def ffn(f, n0, n1):
                modulated(2 * f)
                dve.wait_ge(s_browd, 16)
                with dve.Fori(0, GB) as i:
                    j0 = 2 * i + FC * f
                    lo("B", n0 + i)
                    if f == 0:
                        ada_vec(2 * i, 0)
                    lo("A", n0 + i + 1)
                    for r in range(2):
                        dve.wait_ge(s_sil, j0 + r + 3)
                        dve.wait_ge(s_up, j0 + r + 1)
                        tt(gut[r], sil[r], bank(2 + r), ALU.mult).then_inc(s_gu, 1)
                        dve.wait_ge(s_guh, j0 + r + 1)
                        o = i * 1024 + SEQ * r
                        tt(gul[:, ds(o, SEQ)], gut[r], guh[:, ds(o, SEQ)].bitcast(f32), ALU.subtract).then_inc(s_gul, 1)
                    if f == 0:
                        ada_vec(2 * i + 1, 2)
                if f == 0:
                    dve.wait_ge(s_modv, ADA_LOOP + 1)
                    gate_of(0, 0.5, 2)

                def down(m, r, last):
                    lo("B", n1 + m)
                    if not last:
                        lo("A", n1 + m + 1)
                    residual(Y_FFN2 * f + m, m, B_Y[r], 2 * f + 1, 2 * f)

                with dve.Fori(0, 3) as i:
                    for r in range(2):
                        down(2 * i + r, r, False)
                down(6, 0, False)
                down(7, 1, True)

            amplitude(0, 1)
            ffn(0, N_FFN1, N_DOWN1)

            def q_lo(p):
                dve.wait_ge(s_qh, p + 1)
                stt(ql[:], bank(B_P), DH ** -0.5, qh[:].bitcast(f32), ALU.mult, ALU.subtract).then_inc(s_qr, 1)

            def k_lo(p):
                dve.wait_ge(s_kh, p + 1)
                tt(kl[:], bank(B_P), kh[:].bitcast(f32), ALU.subtract).then_inc(s_kr, 1)

            def v_lo(p):
                dve.wait_ge(s_vh, p + 1)
                tt(vpl[:, :, 0:3:2, :], by_token, vph[:, :, 0:3:2, :].bitcast(f32), ALU.subtract).then_inc(s_vr, 1)

            def stick_abs(h, r):
                dve.wait_ge(s_s, h + 1)
                for e, z in two(E[r], B_Z[r]):
                    last = nc.vector.tensor_scalar(e.bitcast(i32), z.bitcast(i32), 0x7FFFFFFF, None, ALU.bitwise_and)
                last.then_inc(s_abs, 1)

            def stick_softplus(h, r):
                dve.wait_ge(s_l, h + 1)
                for e, z in two(E[r], B_Z[r]):
                    last = stt(e, z, 0.0, e, ALU.max, ALU.add)
                last.then_inc(s_sp, 1)

            def stick_lo(h, r):
                dve.wait_ge(s_wh, h + 1)
                tt(wtl[:], E[r][:], wth[:].bitcast(f32), ALU.subtract).then_inc(s_wlo, 1)

            def dil_scores(h, r):
                dve.wait_ge(s_s, h + 1)
                dve.wait_ge(s_tbl[r], 8 * (h - r) - 16 * N_SB + 16)
                nc.vector.memset(carrier[:], 0.0)
                for n in range(NB):
                    b, o = PB[n]
                    last = nc.vector.tensor_tensor_reduce(
                        out=part(E[r], n), in0=ps[:, B_Z[r] + b, o:o + WID[n]], in1=tbl[r][:, P * n:SEQ],
                        scale=1.0, scalar=-3.0e38, op0=ALU.add, op1=ALU.max, accum_out=stats[:, r, 0, n:n + 1])
                last.then_inc(s_zt, 1)
                dve.wait_ge(s_zt, h - H0 + 1)
                nc.vector.tensor_scalar(stats[:, r, 1, :], stats[:, r, 0, :], -1.0, None, ALU.mult).then_inc(s_nm, 1)

            def dil_normal(h, r):
                dve.wait_ge(s_ex, h - H0 + 1)
                nc.vector.reciprocal(stats[:, r, 3, :], stats[:, r, 2, :]).then_inc(s_rd, 1)
                dve.wait_ge(s_rd, h - H0 + 1)
                for n in range(NB):
                    last = nc.vector.tensor_scalar(part(E[r], n), part(E[r], n), stats[:, r, 3, n:n + 1], None, ALU.mult)
                last.then_inc(s_pn, 1)

            def dil_lo(h, r):
                dve.wait_ge(s_wh, h + 1)
                for (l, z), (w, _) in zip(two(wtl, B_Z[r]), two(wth, B_Z[r])):
                    last = tt(l, z, w.bitcast(f32), ALU.subtract)
                last.then_inc(s_wlo, 1)

            def head_out(p):
                dve.wait_ge(s_ors, p + 1)
                stt(sil[0], bank(B_O), vecs[:, ds(p + 112, 1)], sil[1], ALU.mult, ALU.mult).then_inc(s_ot, 1)
                dve.wait_ge(s_oh, p + 1)
                o = ds(p * SEQ, SEQ)
                tt(oTl[:, o], sil[0], oTh[:, o].bitcast(f32), ALU.subtract).then_inc(s_ol, 1)

            def mix_pair(p, dil, proj):
                h = 2 * p
                if proj:
                    lo("q", p + 1)
                (dil_scores if dil else stick_abs)(h, 0)
                if proj:
                    lo("k", p + 1)
                if dil:
                    dil_scores(h + 1, 1)
                    dil_normal(h, 0)
                    dil_normal(h + 1, 1)
                else:
                    stick_softplus(h, 0)
                    stick_abs(h + 1, 1)
                    stick_softplus(h + 1, 1)
                if proj:
                    q_lo(p + 1)
                    lo("v", p + 1)
                (dil_lo if dil else stick_lo)(h, 0)
                if proj:
                    k_lo(p + 1)
                (dil_lo if dil else stick_lo)(h + 1, 1)
                if proj:
                    v_lo(p + 1)
                head_out(p)

            for name in "qkv":
                lo(name, 0)
            amplitude(1, 3)
            gate_of(1, 1.0, 4)
            modulated(1)
            q_lo(0)
            k_lo(0)
            v_lo(0)
            with dve.Fori(0, N_SB) as p:
                mix_pair(p, False, True)
            with dve.Fori(N_SB, PAIRS - 1) as p:
                mix_pair(p, True, True)
            mix_pair(PAIRS - 1, True, False)

            lo("A", N_OUT)
            with dve.Fori(0, 2) as i:
                lo("B", N_OUT + i)
                for r in range(4):
                    residual(4 * i + r + Y_OUT, 4 * i + r, B_Y[r % 2], 2, 1)
                    if r < 3:
                        ada_vec(3 * i + r + ADA_LOOP, 2 * r)
                    if r == 1:
                        lo("A", N_OUT + i + 1)
            dve.wait_ge(s_modv, ADA_LOOP + ADA_OUT + 1)
            amplitude(2, 5)
            gate_of(2, 0.5, 6)
            ffn(1, N_FFN2, N_DOWN2)

            dve.wait_ge(s_rstd, 4)
            for ch in range(KC):
                if ch >= 2:
                    dve.wait_ge(s_ft, ch - 1)
                stt(sil[ch % 2], X(ch), vecs[:, 104 + ch:105 + ch], ssum, ALU.mult, ALU.mult).then_inc(s_fy, 1)

        @block.tensor
        def _(pe):
            mm = nc.tensor.matmul

            def product(dst, w_h, w_l, a_h, a_l, start, stop):
                mm(dst, w_h, a_h, start=start, stop=False, skip_group_check=True)
                mm(dst, w_h, a_l, start=False, stop=False, skip_group_check=True)
                return mm(dst, w_l, a_h, start=False, stop=stop, skip_group_check=True)

            def tile(name, t, cols, col):
                s = slots[name]
                o = t * cols + col
                return s["hi"][:, o:o + P], s["lo"][:, o:o + P]

            pe.sem_inc(s_avh, 1)
            pe.sem_inc(s_tr, 1)
            pe.sem_inc(s_adam, 1)

            pe.wait_ge(s_vec, 128)
            pe.wait_ge(s_maskr, 1)
            nc.tensor.transpose(ps[:, 4, 0:120], rows[0:120, :], ident[0:120, 0:120]).then_inc(s_vect, 1)
            pe.wait_ge(s_x, 16)
            for ch in range(KC):
                if ch >= 2:
                    pe.wait_ge(s_xev, ch - 1)
                for b in range(NB):
                    last = nc.tensor.transpose(ps[:, ch % 2, P * b:P * b + P], x_nat[:, b, P * ch:P * ch + P], ident[:])
                last.then_inc(s_xt, 1)
            pe.wait_ge(s_oneh, 32)
            mm(ps[0:8, 2, :], rel[0:33, 0:8], oneh[0:33, 0:512], start=True, stop=True)
            mm(ps[0:8, 3, 0:128], rel[0:33, 0:8], oneh[0:33, 512:640], start=True, stop=True).then_inc(s_brow, 1)
            pe.wait_ge(s_ones, 1)

            def stat(k):
                pe.wait_ge(s_ssum, 9 * k + 9)
                mm(bank(B_ST), ones[:], ssum, start=True, stop=True).then_inc(s_stat, 1)

            def ada_columns(a, col):
                for e in range(2):
                    last = mm(ps[:, B_MOD, col + e:col + e + 1], a[:, 0, P * e:P * e + P], ones[:, 0:1],
                              start=True, stop=True)
                return last

            stat(0)
            for b in range(ADA_FIRST):
                if b in ADA_POOL:
                    pe.wait_ge(s_sump, ADA_POOL.index(b) + 1)
                else:
                    pe.wait_ge(s_sumv, ADA_DVE.index(b) + 1)
                last = ada_columns(ada0[b], 2 * b)
            last.then_inc(s_mod0, 1)

            def ada_block(n, col):
                pe.wait_ge(s_adap, n + 1)
                pe.wait_ge(s_modv, n + 1)
                ada_columns(ada, col).then_inc(s_adam, 1)

            def ffn(f, n0, n1):
                with pe.Fori(0, GB) as i:
                    j0 = 2 * i + FC * f
                    for name, free, done, b0 in (("A", s_sil, s_gate, 0), ("B", s_gu, s_up, 2)):
                        pe.wait_ge(slots[name]["split"], n0 + i + 2)
                        for r in range(2):
                            pe.wait_ge(free, j0 + r + 1)
                            for k in range(KC):
                                if name == "A" and r == 0:
                                    pe.wait_ge(s_hl, 16 * f + k + 1)
                                w_h, w_l = tile(name, k, 256, P * r)
                                last = product(bank(b0 + r), w_h, w_l, hh[:, k, :], hl[:, k, :], k == 0, k == KC - 1)
                            last.then_inc(done, 1)
                        if f == 0:
                            ada_block(2 * i + (name == "B"), 2 * (name == "B"))
                with pe.Fori(0, 4) as i:
                    for r in range(2):
                        m = 2 * i + r
                        pe.wait_ge(s_xn, m + Y_FFN2 * f + 1)
                        for n, name in enumerate("AB"):
                            pe.wait_ge(slots[name]["split"], n1 + m + 2)
                            pe.wait_ge(s_gul, FC * f + 11 * n + 11)
                            for k in range(11):
                                w_h, w_l = tile(name, k, P, 0)
                                o = SEQ * (11 * n + k)
                                last = product(bank(B_Y[r]), w_h, w_l, guh[:, o:o + SEQ], gul[:, o:o + SEQ],
                                               n == 0 and k == 0, n == 1 and k == 10)
                            if n == 0:
                                last.then_inc(s_half, 1)
                        last.then_inc(s_y, 1)
                stat(2 * f + 1)

            ffn(0, N_FFN1, N_DOWN1)

            def project(name, p, free, count, done):
                pe.wait_ge(slots[name]["split"], p + 2)
                if free is not None:
                    pe.wait_ge(free, count)
                for k in range(KC):
                    if name == "q" and free is None:
                        pe.wait_ge(s_hl, KC + k + 1)
                    w_h, w_l = tile(name, k, P, 0)
                    last = product(bank(B_P), w_h, w_l, hh[:, k, :], hl[:, k, :], k == 0, k == KC - 1)
                last.then_inc(done, 1)

            def values_by_token(p):
                pe.wait_ge(s_vsb, p + 1)
                for b in range(NB):
                    last = nc.tensor.transpose(ps[:, B_P, P * b:P * b + P], vsb[:, P * b:P * b + P], ident[:])
                last.then_inc(s_vt, 1)

            def stick_scores(h, r):
                f = slice(DH * r, DH * r + DH)
                for j in range(NB):
                    b, o = PB[j]
                    dst = ps[:, B_Z[r] + b, o:o + WID[j]]
                    keys, queries = slice(P * j, P * j + P), slice(P * j, SEQ)
                    product(dst, kh[f, keys], kl[f, keys], qh[f, queries], ql[f, queries], j < 3, False)
                    last = mm(ps[:, B_Z[r] + b, o:o + P], ident_r, negm, start=False, stop=True, skip_group_check=True)
                last.then_inc(s_s, 1)

            def stick_suffix(h, r):
                pe.wait_ge(s_spl, h + 1)
                for j in range(NB):
                    b, o = PB[j]
                    for jj in range(j, NB):
                        dst = ps[:, B_Z[r] + b, o + P * (jj - j):o + WID[j]]
                        for t in (sph, spl):
                            last = mm(dst, ntri if jj == j else nones, part(t, jj), start=False, stop=True,
                                      skip_group_check=True)
                last.then_inc(s_tr, 1)

            def dil_scores(h, r):
                f = slice(DH * r, DH * r + DH)
                for n in range(NB):
                    b, o = PB[n]
                    i = NB - 1 - n
                    qs, keys = slice(P * i, P * i + P), slice(0, WID[n])
                    last = product(ps[:, B_Z[r] + b, o:o + WID[n]], qh[f, qs], ql[f, qs], kh[f, keys], kl[f, keys],
                                   n < 3, True)
                last.then_inc(s_s, 1)

            def dil_transpose(h, r):
                pe.wait_ge(s_pn, h - H0 + 1)
                for i in range(NB):
                    for j in range(i + 1):
                        b, o = PB[j]
                        src = E[r][:, OFF[NB - 1 - i] + P * j:OFF[NB - 1 - i] + P * j + P]
                        o += P * (i - j)
                        last = nc.tensor.transpose(ps[:, B_Z[r] + b, o:o + P], src, ident[:])
                last.then_inc(s_tr, 1)

            def attend(h, r):
                pe.wait_ge(s_wlo, h + 3)
                for j in range(NB):
                    v_h, v_l = (v[:, j].rearrange("p e n -> p (e n)")[:, DH * r:DH * r + P] for v in (vph, vpl))
                    last = product(ps[:, B_O, P * j:SEQ], v_h, v_l, part(wth, j), part(wtl, j), r == 0 and j == 0,
                                   j == NB - 1)
                last.then_inc(s_avh, 1)

            def mix_pair(p, dil, proj):
                h = 2 * p
                for r in range(2):
                    pe.wait_ge(s_qr, p + 1)
                    pe.wait_ge(s_kr, p + 1)
                    pe.wait_ge(s_wlo, h + r + 1)
                    (dil_scores if dil else stick_scores)(h + r, r)
                if proj:
                    project("q", p + 1, s_oln, p + 1, s_pq)
                (dil_transpose if dil else stick_suffix)(h, 0)
                if proj:
                    project("k", p + 1, s_qr, p + 2, s_pk)
                pe.wait_ge(s_vr, p + 1)
                pe.wait_ge(s_ot, p + 1)
                attend(h, 0)
                (dil_transpose if dil else stick_suffix)(h + 1, 1)
                if proj:
                    project("v", p + 1, s_kr, p + 2, s_pv)
                attend(h + 1, 1)
                if proj:
                    values_by_token(p + 1)
                    pe.wait_ge(s_vr, p + 2)
                pe.wait_ge(s_osq, p + 1)
                mm(bank(B_P), halves[:], gut[0], start=True, stop=True).then_inc(s_ost, 1)

            project("q", 0, None, 0, s_pq)
            project("k", 0, s_qr, 1, s_pk)
            project("v", 0, s_kr, 1, s_pv)
            values_by_token(0)
            with pe.Fori(0, N_SB) as p:
                mix_pair(p, False, True)
            with pe.Fori(N_SB, PAIRS - 1) as p:
                mix_pair(p, True, True)
            mix_pair(PAIRS - 1, True, False)

            pe.wait_ge(s_ol, PAIRS)
            with pe.Fori(0, 2) as i:
                for r in range(4):
                    name = "AABB"[r]
                    pe.wait_ge(slots[name]["split"], N_OUT + i + 2)
                    pe.wait_ge(s_xn, 4 * i + r + Y_OUT + 1)
                    for k in range(KC):
                        w_h, w_l = tile(name, k, 256, P * (r % 2))
                        o = SEQ * k
                        last = product(bank(B_Y[r % 2]), w_h, w_l, oTh[:, o:o + SEQ], oTl[:, o:o + SEQ], k == 0,
                                       k == KC - 1)
                    last.then_inc(s_y, 1)
                    if r < 3:
                        ada_block(3 * i + r + ADA_LOOP, 2 * r)
            stat(2)
            ffn(1, N_FFN2, N_DOWN2)

            for ch in range(KC):
                pe.wait_ge(s_fy, ch + 1)
                if ch >= 2:
                    pe.wait_ge(s_fo, ch - 1)
                for b in range(NB):
                    last = nc.tensor.transpose(ps[:, ch % 2, P * b:P * b + P], sil[ch % 2][:, P * b:P * b + P], ident[:])
                last.then_inc(s_ft, 1)


_INS = ["x", "c", "w_ada", "b_ada", "g_ffn1", "w1_gate", "w1_up", "w1_down", "g_mix", "w_in", "g_sb_out", "g_dil_out",
        "w_out", "rel_bias", "g_ffn2", "w2_gate", "w2_up", "w2_down", "g_final"]


def _shape_constants():
    import math
    k, q = np.arange(P)[:, None], np.arange(P)[None, :]
    masks = np.stack([
        (k == q).astype(np.float32),
        -(k >= q).astype(np.float32),
        -np.ones((P, P), np.float32),
        np.where(k < q, 0, NEG).astype(np.float32),
        (k // DH == q // DH).astype(np.float32),
    ])
    n = SEQ - 1 - np.arange(ROW)
    near = np.maximum(n, 0)
    large = 16 + (np.log(np.maximum(near, 1).astype(np.float32) / 16) / math.log(2048 / 16) * 16).astype(np.int32)
    bucket = np.where(near < 16, near, np.minimum(large, 31))
    times = (n <= 128).astype(int) + (n % 4 == 0) + (n % 16 == 0)
    times = np.where(n >= 0, times, 0)
    onehot = np.zeros((33, ROW), np.float32)
    onehot[bucket, np.arange(ROW)] = 1
    onehot[32] = np.where(times > 0, np.log(np.maximum(times, 1)), NEG)
    return masks, onehot


def kernel(**inputs):
    import concourse.bacc as bacc
    from concourse.bass_utils import run_bass_kernel_spmd

    nc = bacc.Bacc("TRN2", target_bir_lowering=False, num_devices=1)
    f32 = mybir.dt.float32
    arrays, args = {}, []
    feeds = [(name, np.ascontiguousarray(inputs[name])) for name in _INS]
    feeds += list(zip(("masks", "onehot"), _shape_constants()))
    for name, a in feeds:
        arrays[f"in_{name}"] = a
        args.append(nc.dram_tensor(f"in_{name}", a.shape, f32, kind="ExternalInput").ap())
    args.append(nc.dram_tensor("bias_rows", (8, ROW), f32, kind="Internal").ap())
    args.append(nc.dram_tensor("bias_copies", (8, P, ROW), f32, kind="Internal").ap())
    args.append(nc.dram_tensor("out_0", (1, SEQ, D), f32, kind="ExternalOutput").ap())
    build(nc, *args)
    r = run_bass_kernel_spmd(nc, [arrays], core_ids=[0])
    return r.results[0]["out_0"]
```

```python
import numpy as np
import concourse.bass as bass
from concourse import mybir
from contextlib import ExitStack

SEQ, D, D_FF, DH = 512, 1024, 2816, 64
P = 128
KC = D // P
FC = D_FF // P
NB = SEQ // P
PAIRS = 8
N_SB = 4
D_GRP = 512
EPS = 1e-6
NEG = -1e30
PACK = sum(SEQ - P * j for j in range(NB))
ROW = 640
ADA_FIRST, ADA_COLS = 8, 256
ADA_BLOCKS = 9 * D // ADA_COLS
ARENA = 2 * FC * SEQ
SLOT = 2048


def build(nc, x, c, w_ada, b_ada, g_ffn1, w1_gate, w1_up, w1_down, g_mix, w_in, g_sb_out, g_dil_out, w_out,
          rel_bias, g_ffn2, w2_gate, w2_up, w2_down, g_final, masks, onehot, bias_rows, bias_copies, out):
    f32, f32r, i32 = mybir.dt.float32, mybir.dt.float32r, mybir.dt.int32
    ALU = mybir.AluOpType
    ACT = mybir.ActivationFunctionType
    ds = bass.ds
    ctx = ExitStack()
    with ctx:
        def sb(name, shape, dt=f32):
            return ctx.enter_context(nc.sbuf_tensor(name, shape, dt))

        def sem(name):
            return ctx.enter_context(nc.semaphore(name))

        xT = sb("xT", [P, KC * SEQ])
        hh = sb("hh", [P, KC, SEQ], f32r)
        hl = sb("hl", [P, KC, SEQ], f32r)
        w_raw = sb("w_raw", [P, 2 * SLOT])
        w_hi = sb("w_hi", [P, 2 * SLOT], f32r)
        w_lo = sb("w_lo", [P, 2 * SLOT], f32r)
        ada = sb("ada", [P, 8, ADA_COLS])
        ada_acc = sb("ada_acc", [P, 2, ADA_COLS])
        sumsq = sb("sumsq", [P, NB])
        tmp = sb("tmp", [P, 5, SEQ])
        ident = sb("ident", [P, P])
        ones = sb("ones", [P, P])
        vecs = sb("vecs", [P, 120])
        mod = sb("mod", [P, 72])
        amp = sb("amp", [P, 3 * KC])
        hgate = sb("hgate", [P, 3 * KC])
        csil = sb("csil", [P, KC])
        eps = sb("eps", [P, 2])
        stats = sb("stats", [P, 2, 4, NB])
        rel = sb("rel", [33, 8])
        carrier = sb("carrier", [P, 1])

        arena_at = (nc.sbuf_base + 31) // 32 * 32
        sb("arena", [P, ARENA])
        at = [0]

        def place(name, shape, dt=f32):
            size = 4 * int(np.prod(shape[1:]))
            assert at[0] + size <= 4 * ARENA
            at[0] += size
            return nc.alloc_sbuf_tensor_at(name, shape, dt, offset=arena_at + at[0] - size)

        x_nat = place("x_nat", [P, NB, D])
        ada0 = [place(f"ada0_{b}", [P, 8, 2, P]) for b in range(ADA_FIRST)]
        rows = place("rows", [P, P])
        maskf = place("maskf", [P, P])
        diag = place("diag", [P, 2, P])
        oneh = place("oneh", [P, ROW])
        brow = place("brow", [P, ROW])
        at[0] = 0
        guh = place("guh", [P, FC * SEQ], f32r)
        gul = place("gul", [P, FC * SEQ], f32r)
        at[0] = 0
        oTh = place("oTh", [P, PAIRS * SEQ], f32r)
        oTl = place("oTl", [P, PAIRS * SEQ], f32r)
        qh, ql = place("qh", [P, SEQ], f32r), place("ql", [P, SEQ], f32r)
        kh, kl = place("kh", [P, SEQ], f32r), place("kl", [P, SEQ], f32r)
        vsb = place("vsb", [P, SEQ])
        vph = place("vph", [P, NB, 3, DH], f32r)
        vpl = place("vpl", [P, NB, 3, DH], f32r)
        E = [place("E0", [P, PACK]), place("E1", [P, PACK])]
        sph, spl = place("sph", [P, PACK], f32r), place("spl", [P, PACK], f32r)
        wth, wtl = place("wth", [P, PACK], f32r), place("wtl", [P, PACK], f32r)
        maskm = place("maskm", [P, 5, P])
        maskr = place("maskr", [P, 4, P], f32r)
        halves = maskm[:, 4, :]
        at[0] = 0
        o_nat = place("o_nat", [P, NB, D])

        sil = [tmp[:, 0, :], tmp[:, 1, :]]
        gut = [tmp[:, 2, :], tmp[:, 3, :]]
        ssum = tmp[:, 4, :]
        adaf = ada[:, :, :].rearrange("p t n -> p (t n)")
        tbl = [adaf[:, SEQ * n:SEQ * n + SEQ] for n in range(2)]
        ident_r, ntri, nones, negm = (maskr[:, n, :] for n in range(4))

        ps = ctx.enter_context(nc.psum_tensor("ps", [P, 8, SEQ], f32))

        def bank(n):
            return ps[:, n, :]

        B_Y, B_MOD, B_ST = (4, 5), 6, 7
        B_MOD0 = (4, 5, 6)
        B_Z, B_O, B_P = (0, 3), 6, 7

        def two(ap, b0):
            return [(ap[:, 0:512], bank(b0)),
                    (ap[:, 512:1280].rearrange("p (b n) -> p b n", b=2), ps[:, b0 + 1:b0 + 3, 0:384])]

        OFF = [0, 512, 896, 1152]
        PB = [(0, 0), (1, 0), (2, 0), (2, 256)]
        WID = [SEQ - P * j for j in range(NB)]
        by_token = bank(B_P).rearrange("p (b e n) -> p b e n", b=NB, e=2)

        s_vec, s_masks, s_x, s_oneh, s_rel1, s_ones = (sem(n) for n in ("s_vec", "s_masks", "s_x", "s_oneh", "s_rel1", "s_ones"))
        s_maskr, s_vect, s_vecs, s_csil, s_eps = (sem(n) for n in ("s_maskr", "s_vect", "s_vecs", "s_csil", "s_eps"))
        s_xt, s_xev, s_brow, s_browc, s_browd = (sem(n) for n in ("s_xt", "s_xev", "s_brow", "s_browc", "s_browd"))
        s_ada0 = [sem(f"s_ada0_{n}") for n in range(ADA_FIRST)]
        s_sump, s_sumv, s_mod0, s_modv0, s_amp = (sem(n) for n in ("s_sump", "s_sumv", "s_mod0", "s_modv0", "s_amp"))
        s_adal = [sem("s_adal0"), sem("s_adal1")]
        s_adah, s_adac, s_adap, s_adam, s_modv = (sem(n) for n in ("s_adah", "s_adac", "s_adap", "s_adam", "s_modv"))
        s_adax, s_adav, s_amp0 = sem("s_adax"), sem("s_adav"), sem("s_amp0")
        s_sumsq, s_diag, s_bcast = sem("s_sumsq"), sem("s_diag"), sem("s_bcast")
        slots = {}
        for name, o, n in (("A", 0, SLOT), ("B", SLOT, SLOT), ("q", 0, 1024), ("k", 1024, 1024), ("v", 2048, 1024)):
            slots[name] = dict(raw=w_raw[:, o:o + n], hi=w_hi[:, o:o + n], lo=w_lo[:, o:o + n],
                               loaded=sem(f"s_loaded_{name}"), his=sem(f"s_hi_{name}"),
                               split=sem(f"s_split_{name}"))
        s_sq, s_ssum, s_stat, s_ln, s_rstd = (sem(n) for n in ("s_sq", "s_ssum", "s_stat", "s_ln", "s_rstd"))
        s_t, s_h, s_hh, s_hl = (sem(n) for n in ("s_t", "s_h", "s_hh", "s_hl"))
        s_gate, s_sil, s_up, s_gu, s_guh, s_gul = (sem(n) for n in ("s_gate", "s_sil", "s_up", "s_gu", "s_guh", "s_gul"))
        s_half, s_y, s_xn = sem("s_half"), sem("s_y"), sem("s_xn")
        s_pq, s_qh, s_qr, s_pk, s_kh, s_kr = (sem(n) for n in ("s_pq", "s_qh", "s_qr", "s_pk", "s_kh", "s_kr"))
        s_pv, s_vsb, s_vt, s_vh, s_vr, s_vz = (sem(n) for n in ("s_pv", "s_vsb", "s_vt", "s_vh", "s_vr", "s_vz"))
        s_s, s_abs, s_e, s_l, s_sp, s_sph, s_spl = (sem(n) for n in ("s_s", "s_abs", "s_e", "s_l", "s_sp", "s_sph", "s_spl"))
        s_tr, s_w, s_wh, s_wlo = (sem(n) for n in ("s_tr", "s_w", "s_wh", "s_wlo"))
        s_avh = sem("s_avh")
        s_tbl = [sem("s_tbl0"), sem("s_tbl1")]
        s_zt, s_nm, s_ex, s_rd, s_pn = (sem(n) for n in ("s_zt", "s_nm", "s_ex", "s_rd", "s_pn"))
        s_osq, s_ost, s_oln, s_ors, s_ot, s_oh, s_ol = (
            sem(n) for n in ("s_osq", "s_ost", "s_oln", "s_ors", "s_ot", "s_oh", "s_ol"))
        s_copies, s_ident = sem("s_copies"), sem("s_ident")
        s_fy, s_ft, s_fo, s_out = sem("s_fy"), sem("s_ft"), sem("s_fo"), sem("s_out")

        N_FFN1, N_DOWN1, N_OUT, N_FFN2, N_DOWN2 = 0, 11, 19, 21, 32
        GB, DB = FC // 2, KC
        ADA_LOOP = ADA_BLOCKS - ADA_FIRST
        ADA_DOWN = ADA_LOOP - 2 * GB
        H0 = 2 * N_SB
        Y_OUT, Y_FFN2 = KC, 2 * KC

        def X(ch):
            return xT[:, SEQ * ch:SEQ * ch + SEQ]

        def part(t, n):
            return t[:, OFF[n]:OFF[n] + WID[n]]

        block = ctx.enter_context(nc.Block())

        @block.sync
        def _(sp):
            wv = w_ada[0].rearrange("(t p) n -> p t n", p=P)

            def load_first(b):
                for m in range(2):
                    sp.dma_start(ada0[b][:, :, m, :], wv[:, :, m * D + P * b:m * D + P * b + P]).then_inc(s_ada0[b], 16)

            def load_ada(n):
                for e, free in enumerate((s_adah, s_adap)):
                    sp.wait_ge(free, n + 1)
                    sp.dma_start(ada[:, 4 * e:4 * e + 4, :], wv[:, 4 * e:4 * e + 4, ds((n + ADA_FIRST) * ADA_COLS, ADA_COLS)]
                                 ).then_inc(s_adal[e], 16)

            def load(name, n, src):
                s = slots[name]
                sp.wait_ge(s["split"], n + 1)
                t, cols = src.shape[1], src.shape[2]
                dst = s["raw"][:, 0:t * cols].rearrange("p (t n) -> p t n", t=t)
                sp.dma_start(dst, src).then_inc(s["loaded"], 16)

            def load_ffn(f, wg, wu, wd, n0, n1):
                g = wg[0].rearrange("(t p) n -> p t n", p=P)
                u = wu[0].rearrange("(t p) n -> p t n", p=P)
                d = wd[0].rearrange("(t p) n -> p t n", p=P)
                if f == 0:
                    sp.wait_ge(s_masks, 16)
                    sp.dma_start(x_nat[:], x[0].rearrange("(b p) d -> p b d", p=P)).then_inc(s_x, 16)
                    load_first(0)
                    load("A", n0, g[:, :, 0:256])
                    load_first(1)
                    load("B", n0, u[:, :, 0:256])
                    for b in range(2, ADA_FIRST):
                        load_first(b)
                    load_ada(0)
                    load_ada(1)
                with sp.Fori(1 - f, GB) as i:
                    load("A", n0 + i, g[:, :, ds(i * 256, 256)])
                    if f == 0:
                        load_ada(2 * i)
                    load("B", n0 + i, u[:, :, ds(i * 256, 256)])
                    if f == 0:
                        load_ada(2 * i + 1)
                with sp.Fori(0, ADA_DOWN) as m:
                    load("A", n1 + m, d[:, 0:11, ds(m * P, P)])
                    load("B", n1 + m, d[:, 11:22, ds(m * P, P)])
                    if f == 0:
                        load_ada(m + 2 * GB)
                for m in range(ADA_DOWN, DB):
                    load("A", n1 + m, d[:, 0:11, m * P:m * P + P])
                    load("B", n1 + m, d[:, 11:22, m * P:m * P + P])

            load_ffn(0, w1_gate, w1_up, w1_down, N_FFN1, N_DOWN1)
            sp.wait_ge(s_browd, 16)
            sp.dma_start(bias_copies, bias_rows.unsqueeze(1).broadcast_to([8, P, ROW])).then_inc(s_copies, 16)
            wi = w_in[0].rearrange("(t p) n -> p t n", p=P)
            sp.wait_ge(slots["A"]["split"], N_OUT + 1)
            sp.wait_ge(slots["B"]["split"], N_OUT + 1)
            with sp.Fori(0, N_SB) as p:
                for j, name in enumerate("qkv"):
                    load(name, p, wi[:, :, ds(p * P + j * D_GRP, P)])

            def load_table(h):
                src = bass.AP(tensor=bias_copies.tensor, offset=(h - H0) * P * ROW + P - 1, ap=[[ROW - 1, P], [1, SEQ]])
                sp.dma_start(tbl[h % 2], src).then_inc(s_tbl[h % 2], 16)

            sp.wait_ge(s_copies, 16)
            sp.wait_ge(s_adap, ADA_LOOP + 1)
            load_table(H0)
            load_table(H0 + 1)
            for p in range(N_SB, PAIRS):
                for j, name in enumerate("qkv"):
                    lo_col = (p - N_SB) * P + (j + 3) * D_GRP
                    load(name, p, wi[:, :, lo_col:lo_col + P])
                if p > N_SB:
                    for h in (2 * p, 2 * p + 1):
                        sp.wait_ge(s_nm, h - H0 - 1)
                        load_table(h)
            for name in "qkv":
                sp.wait_ge(slots[name]["split"], PAIRS + 1)
            wo = w_out[0].rearrange("(t p) n -> p t n", p=P)
            with sp.Fori(0, 2) as i:
                load("A", N_OUT + i, wo[:, :, ds(i * 512, 256)])
                load("B", N_OUT + i, wo[:, :, ds(i * 512 + 256, 256)])
            load_ffn(1, w2_gate, w2_up, w2_down, N_FFN2, N_DOWN2)
            ov = out[0].rearrange("(b p) d -> p b d", p=P)
            for n in range(4):
                sp.wait_ge(s_fo, 2 * n + 2)
                sp.dma_start(ov[:, :, 256 * n:256 * n + 256], o_nat[:, :, 256 * n:256 * n + 256]).then_inc(s_out, 16)
            sp.wait_ge(s_out, 64)

        ADA_POOL, ADA_DVE = (0, 2, 4, 6), (1, 3, 5, 7)

        @block.gpsimd
        def _(pool):
            pool.sem_inc(s_adah, 1)
            pool.sem_inc(s_adap, 1)
            nc.gpsimd.memset(rel[:], 1.0).then_inc(s_rel1, 1)
            nc.gpsimd.memset(ones[:], 1.0).then_inc(s_ones, 1)
            nc.gpsimd.memset(eps[:, 0:1], EPS).then_inc(s_eps, 1)
            nc.gpsimd.memset(eps[:, 1:2], 1.0).then_inc(s_eps, 1)

            tt = nc.gpsimd.tensor_tensor

            def times_c(a, t, n):
                return tt(a, a, csil[:, t:t + n].unsqueeze(2).broadcast_to([P, n, ADA_COLS]), ALU.mult)

            pool.wait_ge(s_csil, 1)
            for n, b in enumerate(ADA_POOL):
                pool.wait_ge(s_ada0[b], 32)
                a = ada0[b][:, :, :, :].rearrange("p t m n -> p t (m n)")
                times_c(a, 0, KC).then_inc(s_adax, 1)
                pool.wait_ge(s_adax, 2 * n + 1)
                tt(a[:, 0:4, :], a[:, 0:4, :], a[:, 4:8, :], ALU.add).then_inc(s_adax, 1)
                pool.wait_ge(s_adax, 2 * n + 2)
                tt(a[:, 0:2, :], a[:, 0:2, :], a[:, 2:4, :], ALU.add).then_inc(s_sump, 1)
            with pool.Fori(0, ADA_LOOP // 2) as i:
                for r in range(2):
                    n = 2 * i + r
                    acc = ada_acc[:, r, :]
                    for e in range(2):
                        a = ada[:, 4 * e:4 * e + 4, :]
                        pool.wait_ge(s_adal[e], 16 * n + 16)
                        times_c(a, 4 * e, 4).then_inc(s_adac, 1)
                        pool.wait_ge(s_adac, 5 * n + 2 * e + 1)
                        tt(a[:, 0:2, :], a[:, 0:2, :], a[:, 2:4, :], ALU.add).then_inc(s_adac, 1)
                        pool.wait_ge(s_adac, 5 * n + 2 * e + 2)
                        if e == 0:
                            pool.wait_ge(s_adam, n + 1)
                            tt(acc, a[:, 0, :], a[:, 1, :], ALU.add).then_inc(s_adah, 1)
                    tt(a[:, 0, :], a[:, 0, :], a[:, 1, :], ALU.add).then_inc(s_adac, 1)
                    pool.wait_ge(s_adac, 5 * n + 5)
                    pool.wait_ge(s_adah, n + 2)
                    tt(acc, acc, a[:, 0, :], ALU.add).then_inc(s_adap, 1)
            pool.wait_ge(s_hl, 2 * KC)
            nc.gpsimd.memset(vph[:].bitcast(f32), 0.0).then_inc(s_vz, 1)
            nc.gpsimd.memset(vpl[:].bitcast(f32), 0.0).then_inc(s_vz, 1)
            with pool.Fori(0, N_SB) as p:
                for r in range(2):
                    h = 2 * p + r
                    pool.wait_ge(s_sp, h + 1)
                    pool.wait_ge(s_tr, h + 1)
                    nc.gpsimd.tensor_tensor(sph[:], E[r][:], ones[:, 0:1].broadcast_to([P, PACK]), ALU.mult).then_inc(s_sph, 1)
                    pool.wait_ge(s_sph, h + 1)
                    nc.gpsimd.tensor_tensor(spl[:], E[r][:], sph[:].bitcast(f32), ALU.subtract).then_inc(s_spl, 1)

        @block.scalar
        def _(act):
            fn = nc.scalar.activation

            def hi(name, n):
                s = slots[name]
                act.wait_ge(s["loaded"], 16 * n + 16)
                fn(s["hi"], s["raw"], ACT.Copy).then_inc(s["his"], 1)

            parts = [(b_ada[0].rearrange("(r n) -> r n", n=P), 0, 72), (c[0].rearrange("(r n) -> r n", n=P), 72, 8),
                     (g_ffn1[0].rearrange("(r n) -> r n", n=P), 80, 8), (g_mix[0].rearrange("(r n) -> r n", n=P), 88, 8),
                     (g_ffn2[0].rearrange("(r n) -> r n", n=P), 96, 8), (g_final.rearrange("(r n) -> r n", n=P), 104, 8),
                     (g_sb_out[0].rearrange("(a b) n -> a (b n)", b=2), 112, 4),
                     (g_dil_out[0].rearrange("(a b) n -> a (b n)", b=2), 116, 4)]
            for src, o, n in parts:
                act.dma_start(rows[o:o + n, :], src).then_inc(s_vec, 16)
            act.dma_start(maskf[:], masks[0]).then_inc(s_masks, 16)
            act.dma_start(oneh[0:33, :], onehot).then_inc(s_oneh, 16)
            act.wait_ge(s_rel1, 1)
            act.dma_start(rel[0:32, :], rel_bias).then_inc(s_oneh, 16)
            act.sem_inc(s_sil, 2)
            act.sem_inc(s_oln, 1)
            act.wait_ge(s_masks, 16)
            fn(ident[:], maskf[:], ACT.Copy).then_inc(s_ident, 1)
            act.wait_ge(s_eps, 2)
            act.wait_ge(s_vecs, 1)
            fn(csil[:], vecs[:, 72:80], ACT.Silu).then_inc(s_csil, 1)
            act.wait_ge(s_x, 16)
            for b in range(NB):
                if b >= 2:
                    act.wait_ge(s_sumsq, b - 1)
                e = 2 * (b % 2)
                fn(tmp[:, e:e + 2, :].rearrange("p a n -> p (a n)"), x_nat[:, b, :], ACT.Square,
                   accum_out=sumsq[:, b:b + 1]).then_inc(s_sumsq, 1)
            for ch in range(KC):
                act.wait_ge(s_xt, ch + 1)
                fn(X(ch), bank(ch % 2), ACT.Copy).then_inc(s_xev, 1)
            act.wait_ge(s_brow, 1)
            fn(brow[0:8, 0:512], ps[0:8, 2, :], ACT.Copy).then_inc(s_browc, 1)
            fn(brow[0:8, 512:640], ps[0:8, 3, 0:128], ACT.Copy).then_inc(s_browc, 1)
            act.wait_ge(s_browc, 2)
            act.dma_start(bias_rows, brow[0:8, :]).then_inc(s_browd, 16)

            def rstd(k):
                nc.scalar.preload_act_table_set("natural_log_exp_and_others")
                if k == 0:
                    act.wait_ge(s_bcast, NB)
                else:
                    act.wait_ge(s_stat, k)
                fn(ssum, bank(B_ST), ACT.Ln, bias=eps[:, 0:1], scale=1.0 / D).then_inc(s_ln, 1)
                act.wait_ge(s_ln, k + 1)
                fn(ssum, ssum, ACT.Exp, scale=-0.5).then_inc(s_rstd, 1)

            def ada_product(n):
                b = ADA_DVE[n]
                act.wait_ge(s_ada0[b], 32)
                for t in range(KC):
                    last = fn(ada0[b][:, t, :, :], ada0[b][:, t, :, :], ACT.Copy, scale=csil[:, t:t + 1])
                last.then_inc(s_adav, 1)

            def modulated(k):
                if k == 0:
                    ada_product(0)
                rstd(k)
                for ch in range(KC):
                    act.wait_ge(s_h, KC * k + ch + 1)
                    fn(hh[:, ch, :], sil[ch % 2], ACT.Copy).then_inc(s_hh, 1)
                    if k == 0 and ch in (0, 2, 4):
                        ada_product(ch // 2 + 1)

            def square(k, ch, buf):
                act.wait_ge(s_xn, KC * (k - 1) + ch + 3)
                act.wait_ge(s_ssum, 9 * (k - 1) + ch)
                fn(gut[buf], xT[:, ds(ch * SEQ, SEQ)], ACT.Square).then_inc(s_sq, 1)

            def ffn(f, n0, n1):
                hi("B", n0)
                modulated(2 * f)
                nc.scalar.preload_act_table_set("silu_and_others")
                with act.Fori(0, GB) as i:
                    j0 = 2 * i + FC * f
                    for r in range(2):
                        act.wait_ge(s_gate, j0 + r + 1)
                        act.wait_ge(s_gu, j0 + r + 1)
                        fn(sil[r], bank(r), ACT.Silu).then_inc(s_sil, 1)
                    hi("A", n0 + i + 1)
                    for r in range(2):
                        act.wait_ge(s_gu, j0 + r + 3)
                        fn(guh[:, ds(i * 1024 + SEQ * r, SEQ)], gut[r], ACT.Copy).then_inc(s_guh, 1)
                    hi("B", n0 + i + 1)

                def down(m, r, last):
                    if not last:
                        act.wait_ge(s_half, KC * f + m + 1)
                        hi("A", n1 + m + 1)
                    square(2 * f + 1, m, r)
                    if not last:
                        hi("B", n1 + m + 1)

                with act.Fori(0, 3) as i:
                    for r in range(2):
                        down(2 * i + r, r, False)
                down(6, 0, False)
                down(7, 1, True)

            hi("A", N_FFN1)
            ffn(0, N_FFN1, N_DOWN1)

            def evac_q(p):
                act.wait_ge(s_pq, p + 1)
                fn(qh[:], bank(B_P), ACT.Copy, scale=DH ** -0.5).then_inc(s_qh, 1)

            def evac_k(p, b=B_P):
                act.wait_ge(s_pk, p + 1)
                fn(kh[:], bank(b), ACT.Copy).then_inc(s_kh, 1)

            def evac_v(p, b=B_P):
                act.wait_ge(s_pv, p + 1)
                fn(vsb[:], bank(b), ACT.Copy).then_inc(s_vsb, 1)
                act.wait_ge(s_vt, p + 1)
                fn(vph[:, :, 0:3:2, :], by_token, ACT.Copy).then_inc(s_vh, 1)

            def stick_softplus(h, r):
                act.wait_ge(s_abs, h + 1)
                fn(E[r][:], E[r][:], ACT.Exp, scale=-1.0).then_inc(s_e, 1)
                act.wait_ge(s_e, h + 1)
                fn(E[r][:], E[r][:], ACT.Ln, bias=eps[:, 1:2]).then_inc(s_l, 1)

            def stick_weights(h, r):
                act.wait_ge(s_tr, h + 2)
                for o, z in two(E[r], B_Z[r]):
                    last = fn(o, z, ACT.Exp)
                last.then_inc(s_w, 1)
                act.wait_ge(s_w, h + 1)
                act.wait_ge(s_avh, h + 1)
                fn(wth[:], E[r][:], ACT.Copy).then_inc(s_wh, 1)

            def dil_exp(h, r):
                act.wait_ge(s_nm, h - H0 + 1)
                for n in range(NB):
                    last = fn(part(E[r], n), part(E[r], n), ACT.Exp, bias=stats[:, r, 1, n:n + 1],
                              accum_out=stats[:, r, 2, n:n + 1])
                last.then_inc(s_ex, 1)

            def dil_weights(h, r):
                act.wait_ge(s_tr, h + 2)
                act.wait_ge(s_avh, h + 1)
                for o, z in two(wth, B_Z[r]):
                    last = fn(o, z, ACT.Copy)
                last.then_inc(s_wh, 1)

            def head_out(p):
                act.wait_ge(s_avh, 2 * p + 3)
                fn(gut[0], bank(B_O), ACT.Square).then_inc(s_osq, 1)
                act.wait_ge(s_ost, p + 1)
                fn(sil[1], bank(B_P), ACT.Ln, bias=eps[:, 0:1], scale=1.0 / DH).then_inc(s_oln, 1)
                act.wait_ge(s_oln, p + 2)
                fn(sil[1], sil[1], ACT.Exp, scale=-0.5).then_inc(s_ors, 1)
                act.wait_ge(s_ot, p + 2)
                fn(oTh[:, ds(p * SEQ, SEQ)], sil[0], ACT.Copy).then_inc(s_oh, 1)

            def mix_pair(p, dil, proj):
                h = 2 * p
                first, second = (dil_exp, dil_weights) if dil else (stick_softplus, stick_weights)
                if proj:
                    hi("q", p + 1)
                first(h, 0)
                if proj:
                    hi("k", p + 1)
                first(h + 1, 1)
                if proj:
                    evac_q(p + 1)
                    hi("v", p + 1)
                second(h, 0)
                if proj:
                    evac_k(p + 1)
                second(h + 1, 1)
                if proj:
                    evac_v(p + 1)
                head_out(p)

            nc.scalar.preload_act_table_set("natural_log_exp_and_others")
            for name in "qkv":
                act.wait_ge(s_half, KC)
                hi(name, 0)
            act.wait_ge(s_stat, 1)
            act.dma_start(maskm[:], masks.rearrange("m p n -> p m n")).then_inc(s_masks, 16)
            modulated(1)
            act.wait_ge(s_masks, 32)
            fn(maskr[:], maskm[:, 0:4, :], ACT.Copy).then_inc(s_maskr, 1)
            evac_q(0)
            evac_k(0, B_O)
            act.wait_ge(s_vz, 2)
            evac_v(0, B_Z[0])
            with act.Fori(0, N_SB) as p:
                mix_pair(p, False, True)
            with act.Fori(N_SB, PAIRS - 1) as p:
                mix_pair(p, True, True)
            mix_pair(PAIRS - 1, True, False)

            hi("A", N_OUT)
            hi("B", N_OUT)
            with act.Fori(0, 1) as i:
                for r in range(4):
                    square(2, 4 * i + r, r % 2)
                    if r == 1:
                        hi("A", N_OUT + i + 1)
                hi("B", N_OUT + i + 1)
            for r in range(4):
                square(2, 4 + r, r % 2)
                if r == 1:
                    hi("A", N_OUT + 2)
            ffn(1, N_FFN2, N_DOWN2)

            rstd(3)
            for ch in range(KC):
                act.wait_ge(s_ft, ch + 1)
                fn(o_nat[:, :, P * ch:P * ch + P], bank(ch % 2).rearrange("p (b n) -> p b n", b=NB),
                   ACT.Copy).then_inc(s_fo, 1)

        @block.vector
        def _(dve):
            tt, stt = nc.vector.tensor_tensor, nc.vector.scalar_tensor_tensor

            def lo(name, n):
                s = slots[name]
                dve.wait_ge(s["his"], n + 1)
                tt(s["lo"], s["raw"], s["hi"].bitcast(f32), ALU.subtract).then_inc(s["split"], 1)

            for s in slots.values():
                dve.sem_inc(s["split"], 1)
            dve.sem_inc(s_xn, 2)
            dve.sem_inc(s_gu, 2)
            dve.sem_inc(s_wlo, 2)
            dve.sem_inc(s_ot, 1)
            dve.sem_inc(s_modv, 1)
            dve.wait_ge(s_vect, 1)
            nc.vector.tensor_copy(vecs[:], ps[:, 4, 0:120]).then_inc(s_vecs, 1)

            for b in range(NB):
                dve.wait_ge(s_sumsq, b + 1)
                if b >= 2:
                    dve.wait_ge(s_bcast, b - 1)
                nc.vector.tensor_scalar(diag[:, b % 2, :], ident[:], sumsq[:, b:b + 1], None, ALU.mult).then_inc(s_diag, 1)

            def add_squares(k, ch, buf):
                dve.wait_ge(s_sq, KC * (k - 1) + ch + 1)
                dve.wait_ge(s_ssum, 9 * (k - 1) + ch + 1)
                tt(ssum, ssum, gut[buf], ALU.add).then_inc(s_ssum, 1)

            def ada_first(n):
                dve.wait_ge(s_adav, n + 1)
                a = ada0[ADA_DVE[n]][:, :, :, :].rearrange("p t m n -> p t (m n)")
                tt(a[:, 0:4, :], a[:, 0:4, :], a[:, 4:8, :], ALU.add).then_inc(s_sumv, 1)
                dve.wait_ge(s_sumv, 2 * n + 1)
                tt(a[:, 0:2, :], a[:, 0:2, :], a[:, 2:4, :], ALU.add).then_inc(s_sumv, 1)

            def mod_first(ch):
                dve.wait_ge(s_mod0, ch + 1)
                tt(mod[:, ch:ch + KC + 1:KC], ps[:, B_MOD0[ch % 3], 0:2], vecs[:, ch:ch + KC + 1:KC], ALU.add).then_inc(s_modv0, 1)
                dve.wait_ge(s_modv0, ch + 1)
                stt(amp[:, ch:ch + 1], mod[:, KC + ch:KC + ch + 1], 1.0, vecs[:, 80 + ch:81 + ch], ALU.add, ALU.mult).then_inc(s_amp0, 1)
                dve.wait_ge(s_amp0, ch + 1)

            def ada_vec(n, col):
                dve.wait_ge(s_adam, n + 3)
                o = 2 * ADA_FIRST + 2 * n
                tt(mod[:, ds(o, 2)], ps[:, B_MOD, col:col + 2], vecs[:, ds(o, 2)], ALU.add).then_inc(s_modv, 1)

            def amplitude(k, count):
                stt(amp[:, KC * k:KC * k + KC], mod[:, 24 * k + 8:24 * k + 16], 1.0, vecs[:, 80 + 8 * k:88 + 8 * k],
                    ALU.add, ALU.mult).then_inc(s_amp, 1)
                dve.wait_ge(s_amp, count)

            def gate_of(k, factor, count):
                nc.vector.tensor_scalar(hgate[:, KC * k:KC * k + KC], mod[:, 24 * k + 16:24 * k + 24], factor, None,
                                        ALU.mult).then_inc(s_amp, 1)
                dve.wait_ge(s_amp, count)

            def modulated(k):
                dve.wait_ge(s_rstd, k + 1)

                def h_lo(ch):
                    dve.wait_ge(s_hh, KC * k + ch + 1)
                    tt(hl[:, ch, :], sil[ch % 2], hh[:, ch, :].bitcast(f32), ALU.subtract).then_inc(s_hl, 1)

                for ch in range(KC):
                    if k == 0:
                        mod_first(ch)
                        dve.wait_ge(s_xev, ch + 1)
                    tt(gut[ch % 2], X(ch), ssum, ALU.mult).then_inc(s_t, 1)
                    dve.wait_ge(s_t, KC * k + ch + 1)
                    nc.vector.tensor_scalar(sil[ch % 2], gut[ch % 2], amp[:, KC * k + ch:KC * k + ch + 1],
                                            mod[:, 24 * k + ch:24 * k + ch + 1], ALU.mult, ALU.add).then_inc(s_h, 1)
                    if k == 0:
                        if ch % 2 == 0:
                            ada_first(ch // 2)
                        h_lo(ch)
                    elif ch >= 1:
                        h_lo(ch - 1)
                if k > 0:
                    h_lo(KC - 1)
                nc.vector.memset(ssum, 0.0).then_inc(s_ssum, 1)

            def residual(y, ch, b, k, g):
                dve.wait_ge(s_y, y + 1)
                xs = xT[:, ds(ch * SEQ, SEQ)]
                stt(xs, bank(b), hgate[:, ds(ch + KC * g, 1)], xs, ALU.mult, ALU.add).then_inc(s_xn, 1)
                add_squares(k, ch, b % 2)

            def ffn(f, n0, n1):
                lo("B", n0)
                modulated(2 * f)
                dve.wait_ge(s_browd, 16)
                with dve.Fori(0, GB) as i:
                    j0 = 2 * i + FC * f
                    lo("A", n0 + i + 1)
                    if f == 0:
                        ada_vec(2 * i, 0)
                    for r in range(2):
                        dve.wait_ge(s_sil, j0 + r + 3)
                        dve.wait_ge(s_up, j0 + r + 1)
                        tt(gut[r], sil[r], bank(2 + r), ALU.mult).then_inc(s_gu, 1)
                        dve.wait_ge(s_guh, j0 + r + 1)
                        o = i * 1024 + SEQ * r
                        tt(gul[:, ds(o, SEQ)], gut[r], guh[:, ds(o, SEQ)].bitcast(f32), ALU.subtract).then_inc(s_gul, 1)
                    lo("B", n0 + i + 1)
                    if f == 0:
                        ada_vec(2 * i + 1, 2)
                if f == 0:
                    dve.wait_ge(s_modv, 2 * GB + 1)
                    gate_of(0, 0.5, 1)

                def down(m, r, last):
                    if not last:
                        lo("A", n1 + m + 1)
                    residual(Y_FFN2 * f + m, m, B_Y[r], 2 * f + 1, 2 * f)
                    if not last:
                        lo("B", n1 + m + 1)

                with dve.Fori(0, 3) as i:
                    for r in range(2):
                        down(2 * i + r, r, False)
                        if f == 0:
                            ada_vec(2 * i + r + 2 * GB, 4 * r)
                down(6, 0, False)
                down(7, 1, True)

            lo("A", N_FFN1)
            ffn(0, N_FFN1, N_DOWN1)

            def q_lo(p):
                dve.wait_ge(s_qh, p + 1)
                stt(ql[:], bank(B_P), DH ** -0.5, qh[:].bitcast(f32), ALU.mult, ALU.subtract).then_inc(s_qr, 1)

            def k_lo(p, b=B_P):
                dve.wait_ge(s_kh, p + 1)
                tt(kl[:], bank(b), kh[:].bitcast(f32), ALU.subtract).then_inc(s_kr, 1)

            def v_lo(p):
                dve.wait_ge(s_vh, p + 1)
                tt(vpl[:, :, 0:3:2, :], by_token, vph[:, :, 0:3:2, :].bitcast(f32), ALU.subtract).then_inc(s_vr, 1)

            def stick_abs(h, r):
                dve.wait_ge(s_s, h + 1)
                for e, z in two(E[r], B_Z[r]):
                    last = nc.vector.tensor_scalar(e.bitcast(i32), z.bitcast(i32), 0x7FFFFFFF, None, ALU.bitwise_and)
                last.then_inc(s_abs, 1)

            def stick_softplus(h, r):
                dve.wait_ge(s_l, h + 1)
                for e, z in two(E[r], B_Z[r]):
                    last = stt(e, z, 0.0, e, ALU.max, ALU.add)
                last.then_inc(s_sp, 1)

            def stick_lo(h, r):
                dve.wait_ge(s_wh, h + 1)
                tt(wtl[:], E[r][:], wth[:].bitcast(f32), ALU.subtract).then_inc(s_wlo, 1)

            def dil_scores(h, r):
                dve.wait_ge(s_s, h + 1)
                dve.wait_ge(s_tbl[r], 8 * (h - r) - 16 * N_SB + 16)
                nc.vector.memset(carrier[:], 0.0)
                for n in range(NB):
                    b, o = PB[n]
                    last = nc.vector.tensor_tensor_reduce(
                        out=part(E[r], n), in0=ps[:, B_Z[r] + b, o:o + WID[n]], in1=tbl[r][:, P * n:SEQ],
                        scale=1.0, scalar=-3.0e38, op0=ALU.add, op1=ALU.max, accum_out=stats[:, r, 0, n:n + 1])
                last.then_inc(s_zt, 1)
                dve.wait_ge(s_zt, h - H0 + 1)
                nc.vector.tensor_scalar(stats[:, r, 1, :], stats[:, r, 0, :], -1.0, None, ALU.mult).then_inc(s_nm, 1)

            def dil_normal(h, r):
                dve.wait_ge(s_ex, h - H0 + 1)
                nc.vector.reciprocal(stats[:, r, 3, :], stats[:, r, 2, :]).then_inc(s_rd, 1)
                dve.wait_ge(s_rd, h - H0 + 1)
                for n in range(NB):
                    last = nc.vector.tensor_scalar(part(E[r], n), part(E[r], n), stats[:, r, 3, n:n + 1], None, ALU.mult)
                last.then_inc(s_pn, 1)

            def dil_lo(h, r):
                dve.wait_ge(s_wh, h + 1)
                for (l, z), (w, _) in zip(two(wtl, B_Z[r]), two(wth, B_Z[r])):
                    last = tt(l, z, w.bitcast(f32), ALU.subtract)
                last.then_inc(s_wlo, 1)

            def head_out(p):
                dve.wait_ge(s_ors, p + 1)
                stt(sil[0], bank(B_O), vecs[:, ds(p + 112, 1)], sil[1], ALU.mult, ALU.mult).then_inc(s_ot, 1)
                dve.wait_ge(s_oh, p + 1)
                o = ds(p * SEQ, SEQ)
                tt(oTl[:, o], sil[0], oTh[:, o].bitcast(f32), ALU.subtract).then_inc(s_ol, 1)

            def mix_pair(p, dil, proj):
                h = 2 * p
                if proj:
                    lo("q", p + 1)
                (dil_scores if dil else stick_abs)(h, 0)
                if proj:
                    lo("k", p + 1)
                if dil:
                    dil_scores(h + 1, 1)
                    dil_normal(h, 0)
                    dil_normal(h + 1, 1)
                else:
                    stick_softplus(h, 0)
                    stick_abs(h + 1, 1)
                    stick_softplus(h + 1, 1)
                if proj:
                    q_lo(p + 1)
                    lo("v", p + 1)
                (dil_lo if dil else stick_lo)(h, 0)
                if proj:
                    k_lo(p + 1)
                (dil_lo if dil else stick_lo)(h + 1, 1)
                if proj:
                    v_lo(p + 1)
                head_out(p)

            for name in "qkv":
                lo(name, 0)
            dve.wait_ge(s_modv, ADA_LOOP + 1)
            amplitude(1, 2)
            gate_of(1, 1.0, 3)
            amplitude(2, 4)
            gate_of(2, 0.5, 5)
            modulated(1)
            q_lo(0)
            k_lo(0, B_O)
            v_lo(0)
            with dve.Fori(0, N_SB) as p:
                mix_pair(p, False, True)
            with dve.Fori(N_SB, PAIRS - 1) as p:
                mix_pair(p, True, True)
            mix_pair(PAIRS - 1, True, False)

            lo("A", N_OUT)
            lo("B", N_OUT)
            with dve.Fori(0, 1) as i:
                for r in range(4):
                    residual(4 * i + r + Y_OUT, 4 * i + r, B_Y[r % 2], 2, 1)
                    if r == 1:
                        lo("A", N_OUT + i + 1)
                lo("B", N_OUT + i + 1)
            for r in range(4):
                residual(Y_OUT + 4 + r, 4 + r, B_Y[r % 2], 2, 1)
                if r == 1:
                    lo("A", N_OUT + 2)
            ffn(1, N_FFN2, N_DOWN2)

            dve.wait_ge(s_rstd, 4)
            for ch in range(KC):
                if ch >= 2:
                    dve.wait_ge(s_ft, ch - 1)
                stt(sil[ch % 2], X(ch), vecs[:, 104 + ch:105 + ch], ssum, ALU.mult, ALU.mult).then_inc(s_fy, 1)

        @block.tensor
        def _(pe):
            mm = nc.tensor.matmul

            def product(dst, w_h, w_l, a_h, a_l, start, stop):
                mm(dst, w_h, a_h, start=start, stop=False, skip_group_check=True)
                mm(dst, w_h, a_l, start=False, stop=False, skip_group_check=True)
                return mm(dst, w_l, a_h, start=False, stop=stop, skip_group_check=True)

            def tile(name, t, cols, col):
                s = slots[name]
                o = t * cols + col
                return s["hi"][:, o:o + P], s["lo"][:, o:o + P]

            pe.sem_inc(s_avh, 1)
            pe.sem_inc(s_tr, 1)
            pe.sem_inc(s_adam, 2)

            pe.wait_ge(s_vec, 128)
            pe.wait_ge(s_ident, 1)
            nc.tensor.transpose(ps[:, 4, 0:120], rows[0:120, :], ident[0:120, 0:120]).then_inc(s_vect, 1)
            pe.wait_ge(s_ones, 1)
            for b in range(NB):
                pe.wait_ge(s_diag, b + 1)
                mm(ps[:, B_ST, P * b:P * b + P], ones[:], diag[:, b % 2, :], start=True, stop=True).then_inc(s_bcast, 1)
            pe.wait_ge(s_x, 16)
            for ch in range(KC):
                if ch >= 2:
                    pe.wait_ge(s_xev, ch - 1)
                for b in range(NB):
                    last = nc.tensor.transpose(ps[:, ch % 2, P * b:P * b + P], x_nat[:, b, P * ch:P * ch + P], ident[:])
                last.then_inc(s_xt, 1)
            pe.wait_ge(s_oneh, 32)
            mm(ps[0:8, 2, :], rel[0:33, 0:8], oneh[0:33, 0:512], start=True, stop=True)
            mm(ps[0:8, 3, 0:128], rel[0:33, 0:8], oneh[0:33, 512:640], start=True, stop=True).then_inc(s_brow, 1)

            def stat(k):
                pe.wait_ge(s_ssum, 9 * k)
                mm(bank(B_ST), ones[:], ssum, start=True, stop=True).then_inc(s_stat, 1)

            def modulation_first(ch):
                if ch in ADA_POOL:
                    pe.wait_ge(s_sump, ADA_POOL.index(ch) + 1)
                else:
                    pe.wait_ge(s_sumv, 2 * ADA_DVE.index(ch) + 2)
                if ch >= 3:
                    pe.wait_ge(s_modv0, ch - 2)
                for m in range(2):
                    for t in range(2):
                        last = mm(ps[:, B_MOD0[ch % 3], m:m + 1], ada0[ch][:, t, m, :], ones[:, 0:1], start=t == 0,
                                  stop=t == 1)
                last.then_inc(s_mod0, 1)

            def ada_block(n, r, col):
                pe.wait_ge(s_adap, n + 2)
                pe.wait_ge(s_modv, n + 1)
                for e in range(2):
                    last = mm(ps[:, B_MOD, col + e:col + e + 1], ada_acc[:, r, P * e:P * e + P], ones[:, 0:1],
                              start=True, stop=True)
                last.then_inc(s_adam, 1)

            def ffn(f, n0, n1):
                for name, free in (("A", s_sil), ("B", s_gu)):
                    pe.wait_ge(slots[name]["split"], n0 + 2)
                    pe.wait_ge(free, FC * f + 2)
                for k in range(KC):
                    if f == 0 and k == 0:
                        pe.wait_ge(s_browc, 2)
                        modulation_first(0)
                        modulation_first(1)
                    if f == 0 and 1 <= k < KC - 1:
                        modulation_first(k + 1)
                    pe.wait_ge(s_hl, 16 * f + k + 1)
                    for n, name in enumerate("AB"):
                        for r in range(2):
                            w_h, w_l = tile(name, k, 256, P * r)
                            last = product(bank(2 * n + r), w_h, w_l, hh[:, k, :], hl[:, k, :], k == 0, k == KC - 1)
                            if k == KC - 1:
                                last.then_inc(s_gate if n == 0 else s_up, 1)
                if f == 0:
                    pe.wait_ge(s_modv0, KC)
                    ada_block(0, 0, 0)
                    ada_block(1, 1, 2)
                with pe.Fori(1, GB) as i:
                    j0 = 2 * i + FC * f
                    for name, free, done, b0 in (("A", s_sil, s_gate, 0), ("B", s_gu, s_up, 2)):
                        pe.wait_ge(slots[name]["split"], n0 + i + 2)
                        for r in range(2):
                            pe.wait_ge(free, j0 + r + 1)
                            for k in range(KC):
                                w_h, w_l = tile(name, k, 256, P * r)
                                last = product(bank(b0 + r), w_h, w_l, hh[:, k, :], hl[:, k, :], k == 0, k == KC - 1)
                            last.then_inc(done, 1)
                        if f == 0:
                            e = int(name == "B")
                            ada_block(2 * i + e, e, 2 * e)

                def down(m, r):
                    pe.wait_ge(s_xn, m + Y_FFN2 * f + 1)
                    for n, name in enumerate("AB"):
                        pe.wait_ge(slots[name]["split"], n1 + m + 2)
                        pe.wait_ge(s_gul, FC * f + 11 * n + 11)
                        for k in range(11):
                            w_h, w_l = tile(name, k, P, 0)
                            o = SEQ * (11 * n + k)
                            last = product(bank(B_Y[r]), w_h, w_l, guh[:, o:o + SEQ], gul[:, o:o + SEQ],
                                           n == 0 and k == 0, n == 1 and k == 10)
                        if n == 0:
                            last.then_inc(s_half, 1)
                    last.then_inc(s_y, 1)

                with pe.Fori(0, ADA_DOWN // 2) as i:
                    for r in range(2):
                        down(2 * i + r, r)
                        if f == 0:
                            ada_block(2 * i + r + 2 * GB, r, 4 * r)
                down(6, 0)
                down(7, 1)
                stat(2 * f + 1)

            ffn(0, N_FFN1, N_DOWN1)

            def project(name, p, free, count, done):
                pe.wait_ge(slots[name]["split"], p + 2)
                pe.wait_ge(free, count)
                for k in range(KC):
                    w_h, w_l = tile(name, k, P, 0)
                    last = product(bank(B_P), w_h, w_l, hh[:, k, :], hl[:, k, :], k == 0, k == KC - 1)
                last.then_inc(done, 1)

            def values_by_token(p):
                pe.wait_ge(s_vsb, p + 1)
                for b in range(NB):
                    last = nc.tensor.transpose(ps[:, B_P, P * b:P * b + P], vsb[:, P * b:P * b + P], ident[:])
                last.then_inc(s_vt, 1)

            def stick_scores(h, r):
                f = slice(DH * r, DH * r + DH)
                for j in range(NB):
                    b, o = PB[j]
                    dst = ps[:, B_Z[r] + b, o:o + WID[j]]
                    keys, queries = slice(P * j, P * j + P), slice(P * j, SEQ)
                    product(dst, kh[f, keys], kl[f, keys], qh[f, queries], ql[f, queries], j < 3, False)
                    last = mm(ps[:, B_Z[r] + b, o:o + P], ident_r, negm, start=False, stop=True, skip_group_check=True)
                last.then_inc(s_s, 1)

            def stick_suffix(h, r):
                pe.wait_ge(s_spl, h + 1)
                for j in range(NB):
                    b, o = PB[j]
                    for jj in range(j, NB):
                        dst = ps[:, B_Z[r] + b, o + P * (jj - j):o + WID[j]]
                        for t in (sph, spl):
                            last = mm(dst, ntri if jj == j else nones, part(t, jj), start=False, stop=True,
                                      skip_group_check=True)
                last.then_inc(s_tr, 1)

            def dil_scores(h, r):
                f = slice(DH * r, DH * r + DH)
                for n in range(NB):
                    b, o = PB[n]
                    i = NB - 1 - n
                    qs, keys = slice(P * i, P * i + P), slice(0, WID[n])
                    last = product(ps[:, B_Z[r] + b, o:o + WID[n]], qh[f, qs], ql[f, qs], kh[f, keys], kl[f, keys],
                                   n < 3, True)
                last.then_inc(s_s, 1)

            def dil_transpose(h, r):
                pe.wait_ge(s_pn, h - H0 + 1)
                for i in range(NB):
                    for j in range(i + 1):
                        b, o = PB[j]
                        src = E[r][:, OFF[NB - 1 - i] + P * j:OFF[NB - 1 - i] + P * j + P]
                        o += P * (i - j)
                        last = nc.tensor.transpose(ps[:, B_Z[r] + b, o:o + P], src, ident[:])
                last.then_inc(s_tr, 1)

            def attend(h, r):
                pe.wait_ge(s_wlo, h + 3)
                for j in range(NB):
                    v_h, v_l = (v[:, j].rearrange("p e n -> p (e n)")[:, DH * r:DH * r + P] for v in (vph, vpl))
                    last = product(ps[:, B_O, P * j:SEQ], v_h, v_l, part(wth, j), part(wtl, j), r == 0 and j == 0,
                                   j == NB - 1)
                last.then_inc(s_avh, 1)

            def mix_pair(p, dil, proj):
                h = 2 * p
                for r in range(2):
                    pe.wait_ge(s_qr, p + 1)
                    pe.wait_ge(s_kr, p + 1)
                    pe.wait_ge(s_wlo, h + r + 1)
                    (dil_scores if dil else stick_scores)(h + r, r)
                if proj:
                    project("q", p + 1, s_oln, p + 1, s_pq)
                (dil_transpose if dil else stick_suffix)(h, 0)
                if proj:
                    project("k", p + 1, s_qr, p + 2, s_pk)
                pe.wait_ge(s_vr, p + 1)
                pe.wait_ge(s_ot, p + 1)
                attend(h, 0)
                (dil_transpose if dil else stick_suffix)(h + 1, 1)
                if proj:
                    project("v", p + 1, s_kr, p + 2, s_pv)
                attend(h + 1, 1)
                if proj:
                    values_by_token(p + 1)
                    pe.wait_ge(s_vr, p + 2)
                pe.wait_ge(s_osq, p + 1)
                mm(bank(B_P), halves, gut[0], start=True, stop=True).then_inc(s_ost, 1)

            for name in "qkv":
                pe.wait_ge(slots[name]["split"], 2)
            for k in range(KC):
                pe.wait_ge(s_hl, KC + k + 1)
                for name, b, done in (("q", B_P, s_pq), ("k", B_O, s_pk), ("v", B_Z[0], s_pv)):
                    w_h, w_l = tile(name, k, P, 0)
                    last = product(bank(b), w_h, w_l, hh[:, k, :], hl[:, k, :], k == 0, k == KC - 1)
                    if k == KC - 1:
                        last.then_inc(done, 1)
            pe.wait_ge(s_kr, 1)
            pe.wait_ge(s_maskr, 1)
            values_by_token(0)
            with pe.Fori(0, N_SB) as p:
                mix_pair(p, False, True)
            with pe.Fori(N_SB, PAIRS - 1) as p:
                mix_pair(p, True, True)
            mix_pair(PAIRS - 1, True, False)

            pe.wait_ge(s_ol, PAIRS)
            with pe.Fori(0, 2) as i:
                for r in range(4):
                    name = "AABB"[r]
                    pe.wait_ge(slots[name]["split"], N_OUT + i + 2)
                    pe.wait_ge(s_xn, 4 * i + r + Y_OUT + 1)
                    for k in range(KC):
                        w_h, w_l = tile(name, k, 256, P * (r % 2))
                        o = SEQ * k
                        last = product(bank(B_Y[r % 2]), w_h, w_l, oTh[:, o:o + SEQ], oTl[:, o:o + SEQ], k == 0,
                                       k == KC - 1)
                    last.then_inc(s_y, 1)
            stat(2)
            ffn(1, N_FFN2, N_DOWN2)

            for ch in range(KC):
                pe.wait_ge(s_fy, ch + 1)
                if ch >= 2:
                    pe.wait_ge(s_fo, ch - 1)
                for b in range(NB):
                    last = nc.tensor.transpose(ps[:, ch % 2, P * b:P * b + P], sil[ch % 2][:, P * b:P * b + P], ident[:])
                last.then_inc(s_ft, 1)


_INS = ["x", "c", "w_ada", "b_ada", "g_ffn1", "w1_gate", "w1_up", "w1_down", "g_mix", "w_in", "g_sb_out", "g_dil_out",
        "w_out", "rel_bias", "g_ffn2", "w2_gate", "w2_up", "w2_down", "g_final"]


def _shape_constants():
    import math
    k, q = np.arange(P)[:, None], np.arange(P)[None, :]
    masks = np.stack([
        (k == q).astype(np.float32),
        -(k >= q).astype(np.float32),
        -np.ones((P, P), np.float32),
        np.where(k < q, 0, NEG).astype(np.float32),
        (k // DH == q // DH).astype(np.float32),
    ])
    n = SEQ - 1 - np.arange(ROW)
    near = np.maximum(n, 0)
    large = 16 + (np.log(np.maximum(near, 1).astype(np.float32) / 16) / math.log(2048 / 16) * 16).astype(np.int32)
    bucket = np.where(near < 16, near, np.minimum(large, 31))
    times = (n <= 128).astype(int) + (n % 4 == 0) + (n % 16 == 0)
    times = np.where(n >= 0, times, 0)
    onehot = np.zeros((33, ROW), np.float32)
    onehot[bucket, np.arange(ROW)] = 1
    onehot[32] = np.where(times > 0, np.log(np.maximum(times, 1)), NEG)
    return masks, onehot


def kernel(**inputs):
    import concourse.bacc as bacc
    from concourse.bass_utils import run_bass_kernel_spmd

    nc = bacc.Bacc("TRN2", target_bir_lowering=False, num_devices=1)
    f32 = mybir.dt.float32
    arrays, args = {}, []
    feeds = [(name, np.ascontiguousarray(inputs[name])) for name in _INS]
    feeds += list(zip(("masks", "onehot"), _shape_constants()))
    for name, a in feeds:
        arrays[f"in_{name}"] = a
        args.append(nc.dram_tensor(f"in_{name}", a.shape, f32, kind="ExternalInput").ap())
    args.append(nc.dram_tensor("bias_rows", (8, ROW), f32, kind="Internal").ap())
    args.append(nc.dram_tensor("bias_copies", (8, P, ROW), f32, kind="Internal").ap())
    args.append(nc.dram_tensor("out_0", (1, SEQ, D), f32, kind="ExternalOutput").ap())
    build(nc, *args)
    r = run_bass_kernel_spmd(nc, [arrays], core_ids=[0])
    return r.results[0]["out_0"]
```

```python
import numpy as np
import concourse.bass as bass
from concourse import mybir
from contextlib import ExitStack

SEQ, D, D_FF, DH = 512, 1024, 2816, 64
P = 128
KC = D // P
FC = D_FF // P
NB = SEQ // P
PAIRS = 8
N_SB = 4
D_GRP = 512
EPS = 1e-6
NEG = -1e30
PACK = sum(SEQ - P * j for j in range(NB))
ROW = 640
ADA_FIRST, ADA_COLS = 8, 256
ADA_BLOCKS = 9 * D // ADA_COLS
ARENA = 2 * FC * SEQ
SLOT = 2048


def build(nc, x, c, w_ada, b_ada, g_ffn1, w1_gate, w1_up, w1_down, g_mix, w_in, g_sb_out, g_dil_out, w_out,
          rel_bias, g_ffn2, w2_gate, w2_up, w2_down, g_final, masks, onehot, bias_rows, bias_copies, out):
    f32, f32r, i32 = mybir.dt.float32, mybir.dt.float32r, mybir.dt.int32
    ALU = mybir.AluOpType
    ACT = mybir.ActivationFunctionType
    ds = bass.ds
    ctx = ExitStack()
    with ctx:
        def sb(name, shape, dt=f32):
            return ctx.enter_context(nc.sbuf_tensor(name, shape, dt))

        def sem(name):
            return ctx.enter_context(nc.semaphore(name))

        xT = sb("xT", [P, KC * SEQ])
        input_at = (nc.sbuf_base + 31) // 32 * 32
        sb("input_region", [P, 2 * KC * SEQ + 8])
        hh = nc.alloc_sbuf_tensor_at("hh", [P, KC, SEQ], f32r, offset=input_at)
        hl = nc.alloc_sbuf_tensor_at("hl", [P, KC, SEQ], f32r, offset=input_at + 4 * KC * SEQ)
        o_nat = nc.alloc_sbuf_tensor_at("o_nat", [P, NB, D], f32, offset=input_at)
        w_raw = sb("w_raw", [P, 2 * SLOT])
        w_hi = sb("w_hi", [P, 2 * SLOT], f32r)
        w_lo = sb("w_lo", [P, 2 * SLOT], f32r)
        ada = sb("ada", [P, 8, ADA_COLS])
        ada_acc = sb("ada_acc", [P, 2, ADA_COLS])
        sumsq = sb("sumsq", [P, NB])
        tmp = sb("tmp", [P, 5, SEQ])
        ident = sb("ident", [P, P])
        ones = sb("ones", [P, P])
        vecs = sb("vecs", [P, 120])
        mod = sb("mod", [P, 72])
        amp = sb("amp", [P, 3 * KC])
        hgate = sb("hgate", [P, 3 * KC])
        csil = sb("csil", [P, KC])
        eps = sb("eps", [P, 2])
        stats = sb("stats", [P, 2, 4, NB])
        rel = sb("rel", [33, 8])
        carrier = sb("carrier", [P, 1])

        arena_at = (nc.sbuf_base + 31) // 32 * 32
        sb("arena", [P, ARENA])
        at = [0]

        def place(name, shape, dt=f32):
            size = 4 * int(np.prod(shape[1:]))
            assert at[0] + size <= 4 * ARENA
            at[0] += size
            return nc.alloc_sbuf_tensor_at(name, shape, dt, offset=arena_at + at[0] - size)

        x_nat = place("x_nat", [P, NB, D])
        ada0 = [place(f"ada0_{b}", [P, 8, 2, P]) for b in range(ADA_FIRST)]
        rows = place("rows", [P, P])
        maskf = place("maskf", [P, P])
        diag = place("diag", [P, 2, P])
        oneh = place("oneh", [P, ROW])
        brow = place("brow", [P, ROW])
        at[0] = 0
        guh = place("guh", [P, FC * SEQ], f32r)
        gul = place("gul", [P, FC * SEQ], f32r)
        at[0] = 0
        oTh = place("oTh", [P, PAIRS * SEQ], f32r)
        oTl = place("oTl", [P, PAIRS * SEQ], f32r)
        qs = [place("qs0", [P, SEQ], f32r), place("qs1", [P, SEQ], f32r)]
        ks = [place("ks0", [P, SEQ], f32r), place("ks1", [P, SEQ], f32r)]
        ql, kl = place("ql", [P, SEQ], f32r), place("kl", [P, SEQ], f32r)
        vsb = place("vsb", [P, SEQ])
        vph = place("vph", [P, NB, 3, DH], f32r)
        vpl = place("vpl", [P, NB, 3, DH], f32r)
        E = [place("E0", [P, PACK]), place("E1", [P, PACK])]
        mh = [place("mh0", [P, PACK], f32r), place("mh1", [P, PACK], f32r)]
        ml = [place("ml0", [P, PACK], f32r), place("ml1", [P, PACK], f32r)]
        maskm = place("maskm", [P, 5, P])
        maskr = place("maskr", [P, 4, P], f32r)
        halves = maskm[:, 4, :]

        sil = [tmp[:, 0, :], tmp[:, 1, :]]
        gut = [tmp[:, 2, :], tmp[:, 3, :]]
        ssum = tmp[:, 4, :]
        adaf = ada[:, :, :].rearrange("p t n -> p (t n)")
        tbl = [adaf[:, SEQ * n:SEQ * n + SEQ] for n in range(2)]
        ident_r, ntri, nones, negm = (maskr[:, n, :] for n in range(4))

        ps = ctx.enter_context(nc.psum_tensor("ps", [P, 8, SEQ], f32))

        def bank(n):
            return ps[:, n, :]

        B_Y, B_MOD, B_ST = (4, 5), 6, 7
        B_MOD0 = (4, 5, 6)
        B_Z, B_O, B_P = (0, 3), 6, 7
        B_OUT = (7, 6, 1, 2, 4, 5, 3, 0)
        B_LAST = 0

        def two(ap, b0):
            return [(ap[:, 0:512], bank(b0)),
                    (ap[:, 512:1280].rearrange("p (b n) -> p b n", b=2), ps[:, b0 + 1:b0 + 3, 0:384])]

        OFF = [0, 512, 896, 1152]
        PB = [(0, 0), (1, 0), (2, 0), (2, 256)]
        WID = [SEQ - P * j for j in range(NB)]
        by_token = bank(B_P).rearrange("p (b e n) -> p b e n", b=NB, e=2)

        s_vec, s_masks, s_x, s_oneh, s_rel1, s_ones = (
            sem(n) for n in ("s_vec", "s_masks", "s_x", "s_oneh", "s_rel1", "s_ones"))
        s_maskr, s_vect, s_vecs, s_csil, s_eps = (sem(n) for n in ("s_maskr", "s_vect", "s_vecs", "s_csil", "s_eps"))
        s_xt, s_brow, s_browc, s_browd = (sem(n) for n in ("s_xt", "s_brow", "s_browc", "s_browd"))
        s_xev = [sem("s_xev0"), sem("s_xev1")]
        s_ada0 = [sem(f"s_ada0_{n}") for n in range(ADA_FIRST)]
        s_sump, s_sumv, s_mod0, s_modv0, s_amp = (sem(n) for n in ("s_sump", "s_sumv", "s_mod0", "s_modv0", "s_amp"))
        s_adal = [sem("s_adal0"), sem("s_adal1")]
        s_adah, s_adac, s_adap, s_adam, s_modv = (sem(n) for n in ("s_adah", "s_adac", "s_adap", "s_adam", "s_modv"))
        s_adax, s_adav, s_amp0 = sem("s_adax"), sem("s_adav"), sem("s_amp0")
        s_sumsq, s_diag, s_bcast = sem("s_sumsq"), sem("s_diag"), sem("s_bcast")
        slots = {}
        for name, o, n in (("A", 0, SLOT), ("B", SLOT, SLOT), ("q", 0, 1024), ("k", 1024, 1024), ("v", 2048, 1024)):
            slots[name] = dict(raw=w_raw[:, o:o + n], hi=w_hi[:, o:o + n], lo=w_lo[:, o:o + n],
                               loaded=sem(f"s_loaded_{name}"), his=sem(f"s_hi_{name}"),
                               split=sem(f"s_split_{name}"))
        s_sq, s_ssum, s_stat, s_ln, s_rstd = (sem(n) for n in ("s_sq", "s_ssum", "s_stat", "s_ln", "s_rstd"))
        s_t, s_hh, s_hl = (sem(n) for n in ("s_t", "s_hh", "s_hl"))
        s_gate, s_sil, s_up, s_gu, s_guh, s_gul = (sem(n) for n in ("s_gate", "s_sil", "s_up", "s_gu", "s_guh", "s_gul"))
        s_half, s_y, s_xn = sem("s_half"), sem("s_y"), sem("s_xn")
        s_pq, s_qh, s_qr, s_pk, s_kh, s_kr = (sem(n) for n in ("s_pq", "s_qh", "s_qr", "s_pk", "s_kh", "s_kr"))
        s_pv, s_vsb, s_vt, s_vh, s_vr, s_vz = (sem(n) for n in ("s_pv", "s_vsb", "s_vt", "s_vh", "s_vr", "s_vz"))
        s_s, s_abs, s_e, s_l, s_sp, s_sph, s_spl = (
            sem(n) for n in ("s_s", "s_abs", "s_e", "s_l", "s_sp", "s_sph", "s_spl"))
        s_tr, s_w, s_wh, s_wlo = (sem(n) for n in ("s_tr", "s_w", "s_wh", "s_wlo"))
        s_avh = sem("s_avh")
        s_tbl = [sem("s_tbl0"), sem("s_tbl1")]
        s_zt, s_nm, s_ex, s_rd, s_pn = (sem(n) for n in ("s_zt", "s_nm", "s_ex", "s_rd", "s_pn"))
        s_osq, s_ost, s_oln, s_ors, s_ot, s_oh, s_ol = (
            sem(n) for n in ("s_osq", "s_ost", "s_oln", "s_ors", "s_ot", "s_oh", "s_ol"))
        s_qd, s_kd = sem("s_qd"), sem("s_kd")
        s_copies, s_ident = sem("s_copies"), sem("s_ident")
        s_fy, s_ft, s_fo, s_out = sem("s_fy"), sem("s_ft"), sem("s_fo"), sem("s_out")
        s_fl, s_fr, s_fs = sem("s_fl"), sem("s_fr"), [sem("s_fs0"), sem("s_fs1")]

        N_FFN1, N_DOWN1, N_OUT, N_FFN2, N_DOWN2 = 0, 11, 19, 21, 32
        GB, DB = FC // 2, KC
        ADA_LOOP = ADA_BLOCKS - ADA_FIRST
        ADA_DOWN = 2 * GB - 2
        assert ADA_LOOP == ADA_DOWN + DB
        H0 = 2 * N_SB
        Y_OUT, Y_FFN2 = KC, 2 * KC

        def X(ch):
            return xT[:, SEQ * ch:SEQ * ch + SEQ]

        own = [slice(0, DH), slice(DH, P)]

        def part(t, n):
            return t[:, OFF[n]:OFF[n] + WID[n]]

        block = ctx.enter_context(nc.Block())

        @block.sync
        def _(sp):
            wv = w_ada[0].rearrange("(t p) n -> p t n", p=P)

            def load_first(b):
                for m in range(2):
                    sp.dma_start(ada0[b][:, :, m, :], wv[:, :, m * D + P * b:m * D + P * b + P]).then_inc(s_ada0[b], 16)

            def load_ada(n):
                for e, free in enumerate((s_adah, s_adap)):
                    sp.wait_ge(free, n + 1)
                    sp.dma_start(ada[:, 4 * e:4 * e + 4, :], wv[:, 4 * e:4 * e + 4, ds((n + ADA_FIRST) * ADA_COLS, ADA_COLS)]
                                 ).then_inc(s_adal[e], 16)

            def load(name, n, src):
                s = slots[name]
                sp.wait_ge(s["split"], n + 1)
                t, cols = src.shape[1], src.shape[2]
                dst = s["raw"][:, 0:t * cols].rearrange("p (t n) -> p t n", t=t)
                sp.dma_start(dst, src).then_inc(s["loaded"], 16)

            def load_ffn(f, wg, wu, wd, n0, n1):
                g = wg[0].rearrange("(t p) n -> p t n", p=P)
                u = wu[0].rearrange("(t p) n -> p t n", p=P)
                d = wd[0].rearrange("(t p) n -> p t n", p=P)
                if f == 0:
                    sp.wait_ge(s_vec, 128)
                    load_first(0)
                    load("A", n0, g[:, :, 0:256])
                    load_first(1)
                    load("B", n0, u[:, :, 0:256])
                    for b in range(2, ADA_FIRST):
                        load_first(b)
                    sp.wait_ge(s_browc, 2)
                    sp.dma_start(bias_rows, brow[0:8, :]).then_inc(s_browd, 16)
                    load_ada(0)
                with sp.Fori(1 - f, GB) as i:
                    load("A", n0 + i, g[:, :, ds(i * 256, 256)])
                    load("B", n0 + i, u[:, :, ds(i * 256, 256)])
                    if f == 0:
                        load_ada(2 * i - 1)
                        load_ada(2 * i)

                def load_down(m):
                    load("A", n1 + m, d[:, 0:11, ds(m * P, P)])
                    load("B", n1 + m, d[:, 11:22, ds(m * P, P)])

                with sp.Fori(0, DB - 1) as m:
                    load_down(m)
                    if f == 0:
                        load_ada(m + ADA_DOWN + 1)
                load_down(DB - 1)

            load_ffn(0, w1_gate, w1_up, w1_down, N_FFN1, N_DOWN1)
            sp.wait_ge(s_browd, 16)
            sp.dma_start(bias_copies, bias_rows.unsqueeze(1).broadcast_to([8, P, ROW])).then_inc(s_copies, 16)
            wi = w_in[0].rearrange("(t p) n -> p t n", p=P)
            sp.wait_ge(slots["A"]["split"], N_OUT + 1)
            sp.wait_ge(slots["B"]["split"], N_OUT + 1)
            with sp.Fori(0, N_SB) as p:
                for j, name in enumerate("qkv"):
                    load(name, p, wi[:, :, ds(p * P + j * D_GRP, P)])

            def load_table(h):
                src = bass.AP(tensor=bias_copies.tensor, offset=(h - H0) * P * ROW + P - 1, ap=[[ROW - 1, P], [1, SEQ]])
                sp.dma_start(tbl[h % 2], src).then_inc(s_tbl[h % 2], 16)

            sp.wait_ge(s_copies, 16)
            sp.wait_ge(s_adap, ADA_LOOP + 1)
            load_table(H0)
            load_table(H0 + 1)
            for p in range(N_SB, PAIRS):
                for j, name in enumerate("qkv"):
                    lo_col = (p - N_SB) * P + (j + 3) * D_GRP
                    load(name, p, wi[:, :, lo_col:lo_col + P])
                if p > N_SB:
                    for h in (2 * p, 2 * p + 1):
                        sp.wait_ge(s_nm, h - H0 - 1)
                        load_table(h)
            for name in "qkv":
                sp.wait_ge(slots[name]["split"], PAIRS + 1)
            wo = w_out[0].rearrange("(t p) n -> p t n", p=P)
            with sp.Fori(0, 2) as i:
                load("A", N_OUT + i, wo[:, :, ds(i * 512, 256)])
                load("B", N_OUT + i, wo[:, :, ds(i * 512 + 256, 256)])
            load_ffn(1, w2_gate, w2_up, w2_down, N_FFN2, N_DOWN2)
            ov = out[0].rearrange("(b p) d -> p b d", p=P)
            for n in range(2):
                for e in (1, 0):
                    b = 2 * e + n
                    sp.wait_ge(s_fs[e], n + 1)
                    sp.dma_start(ov[:, b, :], o_nat[:, b, :]).then_inc(s_out, 16)
            sp.wait_ge(s_out, 64)

        ADA_POOL, ADA_DVE = (0, 1, 3, 5, 7), (2, 4, 6)

        @block.gpsimd
        def _(pool):
            pool.sem_inc(s_adah, 1)
            pool.sem_inc(s_adap, 1)
            nc.gpsimd.memset(rel[:], 1.0).then_inc(s_rel1, 1)
            nc.gpsimd.memset(ones[:], 1.0).then_inc(s_ones, 1)
            nc.gpsimd.memset(eps[:, 0:1], EPS).then_inc(s_eps, 1)
            nc.gpsimd.memset(eps[:, 1:2], 1.0).then_inc(s_eps, 1)

            tt = nc.gpsimd.tensor_tensor

            def times_c(a, t, n):
                return tt(a, a, csil[:, t:t + n].unsqueeze(2).broadcast_to([P, n, ADA_COLS]), ALU.mult)

            pool.wait_ge(s_csil, 1)
            for n, b in enumerate(ADA_POOL):
                pool.wait_ge(s_ada0[b], 32)
                a = ada0[b][:, :, :, :].rearrange("p t m n -> p t (m n)")
                times_c(a, 0, KC).then_inc(s_adax, 1)
                pool.wait_ge(s_adax, 2 * n + 1)
                tt(a[:, 0:4, :], a[:, 0:4, :], a[:, 4:8, :], ALU.add).then_inc(s_adax, 1)
                pool.wait_ge(s_adax, 2 * n + 2)
                tt(a[:, 0:2, :], a[:, 0:2, :], a[:, 2:4, :], ALU.add).then_inc(s_sump, 1)
            with pool.Fori(0, ADA_LOOP // 2) as i:
                for r in range(2):
                    n = 2 * i + r
                    acc = ada_acc[:, r, :]
                    for e in range(2):
                        a = ada[:, 4 * e:4 * e + 4, :]
                        pool.wait_ge(s_adal[e], 16 * n + 16)
                        times_c(a, 4 * e, 4).then_inc(s_adac, 1)
                        pool.wait_ge(s_adac, 5 * n + 2 * e + 1)
                        tt(a[:, 0:2, :], a[:, 0:2, :], a[:, 2:4, :], ALU.add).then_inc(s_adac, 1)
                        pool.wait_ge(s_adac, 5 * n + 2 * e + 2)
                        if e == 0:
                            pool.wait_ge(s_adam, n + 1)
                            tt(acc, a[:, 0, :], a[:, 1, :], ALU.add).then_inc(s_adah, 1)
                    tt(a[:, 0, :], a[:, 0, :], a[:, 1, :], ALU.add).then_inc(s_adac, 1)
                    pool.wait_ge(s_adac, 5 * n + 5)
                    pool.wait_ge(s_adah, n + 2)
                    tt(acc, acc, a[:, 0, :], ALU.add).then_inc(s_adap, 1)
            def lo(name, p):
                s = slots[name]
                pool.wait_ge(s["his"], p + 1)
                tt(s["lo"], s["raw"], s["hi"].bitcast(f32), ALU.subtract).then_inc(s["split"], 1)

            for name in "qkv":
                lo(name, 0)
            pool.wait_ge(s_stat, 1)
            nc.gpsimd.memset(vph[:].bitcast(f32), 0.0).then_inc(s_vz, 1)
            nc.gpsimd.memset(vpl[:].bitcast(f32), 0.0).then_inc(s_vz, 1)

            def copy_q():
                for r in range(2):
                    pool.dma_start(qs[r][own[1 - r], :], qs[r][own[r], :]).then_inc(s_qd, 16)

            def copy_k():
                for r in range(2):
                    pool.dma_start(ks[r][own[1 - r], :], kl[own[r], :]).then_inc(s_kd, 16)

            pool.wait_ge(s_qh, 1)
            copy_q()
            pool.wait_ge(s_kr, 1)
            copy_k()
            for name in "qkv":
                lo(name, 1)
            with pool.Fori(1, PAIRS - 1) as p:
                lo("q", p + 1)
                copy_q()
                pool.wait_ge(s_kr, p + 1)
                lo("k", p + 1)
                copy_k()
                lo("v", p + 1)
            pool.wait_ge(s_qh, PAIRS)
            copy_q()
            pool.wait_ge(s_kr, PAIRS)
            copy_k()
            lo("B", N_FFN2)

        @block.scalar
        def _(act):
            fn = nc.scalar.activation

            def hi(name, n):
                s = slots[name]
                act.wait_ge(s["loaded"], 16 * n + 16)
                fn(s["hi"], s["raw"], ACT.Copy).then_inc(s["his"], 1)

            parts = [(b_ada[0].rearrange("(r n) -> r n", n=P), 0, 72), (c[0].rearrange("(r n) -> r n", n=P), 72, 8),
                     (g_ffn1[0].rearrange("(r n) -> r n", n=P), 80, 8), (g_mix[0].rearrange("(r n) -> r n", n=P), 88, 8),
                     (g_ffn2[0].rearrange("(r n) -> r n", n=P), 96, 8), (g_final.rearrange("(r n) -> r n", n=P), 104, 8),
                     (g_sb_out[0].rearrange("(a b) n -> a (b n)", b=2), 112, 4),
                     (g_dil_out[0].rearrange("(a b) n -> a (b n)", b=2), 116, 4)]
            act.dma_start(maskf[:], masks[0]).then_inc(s_masks, 16)
            act.dma_start(x_nat[:], x[0].rearrange("(b p) d -> p b d", p=P)).then_inc(s_x, 16)
            for src, o, n in parts:
                act.dma_start(rows[o:o + n, :], src).then_inc(s_vec, 16)
            act.dma_start(oneh[0:33, :], onehot).then_inc(s_oneh, 16)
            act.wait_ge(s_rel1, 1)
            act.dma_start(rel[0:32, :], rel_bias).then_inc(s_oneh, 16)
            act.sem_inc(s_sil, 2)
            act.sem_inc(s_fo, 2)
            act.sem_inc(s_oln, 1)
            act.wait_ge(s_masks, 16)
            fn(ident[:], maskf[:], ACT.Copy).then_inc(s_ident, 1)
            act.wait_ge(s_eps, 2)
            act.wait_ge(s_vecs, 1)
            fn(csil[:], vecs[:, 72:80], ACT.Silu).then_inc(s_csil, 1)

            def rstd(k):
                if k == 0:
                    act.wait_ge(s_bcast, NB)
                else:
                    act.wait_ge(s_stat, k)
                fn(ssum, bank(B_ST), ACT.Ln, bias=eps[:, 0:1], scale=1.0 / D).then_inc(s_ln, 1)
                act.wait_ge(s_ln, k + 1)
                fn(ssum, ssum, ACT.Exp, scale=-0.5).then_inc(s_rstd, 1)

            act.wait_ge(s_x, 16)
            for b in range(NB):
                if b >= 2:
                    act.wait_ge(s_sumsq, b - 1)
                e = 2 * (b % 2)
                fn(tmp[:, e:e + 2, :].rearrange("p a n -> p (a n)"), x_nat[:, b, :], ACT.Square,
                   accum_out=sumsq[:, b:b + 1]).then_inc(s_sumsq, 1)
            nc.scalar.preload_act_table_set("natural_log_exp_and_others")
            rstd(0)
            for ch in range(0, KC, 2):
                act.wait_ge(s_xt, ch + 1)
                fn(X(ch), bank(0), ACT.Copy).then_inc(s_xev[0], 1)

            def ada_product(n):
                b = ADA_DVE[n]
                act.wait_ge(s_ada0[b], 32)
                for t in range(KC):
                    last = fn(ada0[b][:, t, :, :], ada0[b][:, t, :, :], ACT.Copy, scale=csil[:, t:t + 1])
                last.then_inc(s_adav, 1)

            def modulated(k):
                if k > 0:
                    rstd(k)
                for ch in range(KC):
                    act.wait_ge(s_t, KC * k + ch + 1)
                    fn(hh[:, ch, :], tmp[:, ch % 4, :], ACT.Identity, bias=mod[:, 24 * k + ch:24 * k + ch + 1]).then_inc(s_hh, 1)
                    if k == 0 and ch == 0:
                        hi("B", N_FFN1)
                    if k == 0 and ch < len(ADA_DVE):
                        ada_product(ch)

            def square(k, ch, buf):
                act.wait_ge(s_xn, KC * (k - 1) + ch + 3)
                act.wait_ge(s_ssum, KC * (k - 1) + ch + 1)
                fn(gut[buf], xT[:, ds(ch * SEQ, SEQ)], ACT.Square).then_inc(s_sq, 1)

            def by_token_out(ch, b):
                act.wait_ge(s_ft, ch + 3)
                fn(o_nat[:, :, ds(P * ch, P)], bank(b).rearrange("p (b n) -> p b n", b=NB), ACT.Copy).then_inc(s_fo, 1)

            def ffn(f, n0, n1):
                if f > 0:
                    hi("B", n0)
                modulated(2 * f)
                nc.scalar.preload_act_table_set("silu_and_others")
                with act.Fori(0, GB) as i:
                    j0 = 2 * i + FC * f
                    for r in range(2):
                        act.wait_ge(s_gate, j0 + r + 1)
                        if r == 1:
                            hi("A", n0 + i + 1)
                        act.wait_ge(s_gu, j0 + r + 1)
                        fn(sil[r], bank(r), ACT.Silu).then_inc(s_sil, 1)
                    for r in range(2):
                        act.wait_ge(s_gu, j0 + r + 3)
                        fn(guh[:, ds(i * 1024 + SEQ * r, SEQ)], gut[r], ACT.Copy).then_inc(s_guh, 1)
                    hi("B", n0 + i + 1)

                def down(m, r, first=False, last=False):
                    act.wait_ge(s_half, KC * f + m + 1)
                    if not last:
                        hi("A", n1 + m + 1)
                    else:
                        if f == 0:
                            hi("q", 0)
                            hi("k", 0)
                        nc.scalar.preload_act_table_set("natural_log_exp_and_others")
                    if f == 1 and not first:
                        by_token_out(m - 1, 1 - r)
                    square(2 * f + 1, m, r)
                    if not last:
                        hi("B", n1 + m + 1)

                down(0, 0, first=True)
                with act.Fori(0, DB // 2 - 1) as i:
                    for r in range(2):
                        down(2 * i + 1 + r, 1 - r)
                down(7, 1, last=True)

            hi("A", N_FFN1)
            ffn(0, N_FFN1, N_DOWN1)

            def evac_q(p):
                act.wait_ge(s_pq, p + 1)
                for r, o in enumerate(own):
                    last = fn(qs[r][o, :], ps[o, B_P, :], ACT.Copy, scale=DH ** -0.5)
                last.then_inc(s_qh, 1)

            def evac_k(p):
                act.wait_ge(s_pk, p + 1)
                for r, o in enumerate(own):
                    last = fn(ks[r][o, :], ps[o, B_O, :], ACT.Copy)
                last.then_inc(s_kh, 1)

            def evac_v(p, b=B_P):
                act.wait_ge(s_pv, p + 1)
                fn(vsb[:], bank(b), ACT.Copy).then_inc(s_vsb, 1)

            def evac_values(p):
                act.wait_ge(s_vt, p + 1)
                fn(vph[:, :, 0:3:2, :], by_token, ACT.Copy).then_inc(s_vh, 1)

            def stick_softplus(h, r):
                act.wait_ge(s_abs, h + 1)
                fn(E[r][:], E[r][:], ACT.Exp, scale=-1.0).then_inc(s_e, 1)
                act.wait_ge(s_e, h + 1)
                fn(E[r][:], E[r][:], ACT.Ln, bias=eps[:, 1:2]).then_inc(s_l, 1)

            def softplus_hi(h, r):
                act.wait_ge(s_sp, h + 1)
                fn(mh[r][:], E[r][:], ACT.Copy).then_inc(s_sph, 1)

            def stick_weights(h, r):
                act.wait_ge(s_tr, h + 1)
                for o, z in two(E[r], B_Z[r]):
                    last = fn(o, z, ACT.Exp)
                last.then_inc(s_w, 1)
                act.wait_ge(s_w, h + 1)
                fn(mh[r][:], E[r][:], ACT.Copy).then_inc(s_wh, 1)

            def dil_exp(h, r):
                act.wait_ge(s_nm, h - H0 + 1)
                for n in range(NB):
                    last = fn(part(E[r], n), part(E[r], n), ACT.Exp, bias=stats[:, r, 1, n:n + 1],
                              accum_out=stats[:, r, 2, n:n + 1])
                last.then_inc(s_ex, 1)

            def dil_weights(h, r):
                act.wait_ge(s_tr, h + 1)
                for o, z in two(mh[r], B_Z[r]):
                    last = fn(o, z, ACT.Copy)
                last.then_inc(s_wh, 1)

            def out_square(p, b=B_O):
                act.wait_ge(s_avh, 2 * p + 2)
                fn(gut[0], bank(b), ACT.Square).then_inc(s_osq, 1)

            def out_rstd(p, b=B_P):
                act.wait_ge(s_ost, p + 1)
                fn(sil[1], bank(b), ACT.Ln, bias=eps[:, 0:1], scale=1.0 / DH).then_inc(s_oln, 1)
                act.wait_ge(s_oln, p + 2)
                fn(sil[1], sil[1], ACT.Exp, scale=-0.5).then_inc(s_ors, 1)

            def out_hi(p):
                act.wait_ge(s_ot, p + 2)
                fn(oTh[:, ds(p * SEQ, SEQ)], sil[0], ACT.Copy).then_inc(s_oh, 1)

            def mix_pair(p, dil, first=False, proj=True, more=True):
                h = 2 * p
                begin, weights = (dil_exp, dil_weights) if dil else (stick_softplus, stick_weights)
                if not first:
                    out_rstd(p - 1)
                begin(h, 0)
                if not first:
                    out_hi(p - 1)
                begin(h + 1, 1)
                if not dil:
                    softplus_hi(h, 0)
                if proj:
                    evac_q(p + 1)
                if not dil:
                    softplus_hi(h + 1, 1)
                if more:
                    hi("q", p + 2)
                if proj:
                    evac_k(p + 1)
                    if more:
                        hi("k", p + 2)
                    else:
                        hi("A", N_OUT)
                weights(h, 0)
                weights(h + 1, 1)
                if proj:
                    evac_v(p + 1)
                    if more:
                        hi("v", p + 2)
                    else:
                        hi("B", N_OUT)
                if proj:
                    evac_values(p + 1)
                out_square(p, B_O if proj else B_LAST)

            hi("v", 0)
            act.wait_ge(s_stat, 1)
            act.dma_start(maskm[:], masks.rearrange("m p n -> p m n")).then_inc(s_masks, 16)
            modulated(1)
            act.wait_ge(s_masks, 32)
            fn(maskr[:], maskm[:, 0:4, :], ACT.Copy).then_inc(s_maskr, 1)
            evac_q(0)
            evac_k(0)
            evac_v(0, B_Z[0])
            act.wait_ge(s_vz, 2)
            evac_values(0)
            for name in "qkv":
                hi(name, 1)
            mix_pair(0, False, first=True)
            with act.Fori(1, N_SB) as p:
                mix_pair(p, False)
            with act.Fori(N_SB, PAIRS - 2) as p:
                mix_pair(p, True)
            mix_pair(PAIRS - 2, True, more=False)
            mix_pair(PAIRS - 1, True, proj=False, more=False)
            out_rstd(PAIRS - 1, B_OUT[5])
            out_hi(PAIRS - 1)

            for ch in range(KC):
                if ch in (1, 3, 5):
                    act.wait_ge(s_y, Y_OUT + ch + 1)
                    hi("ABA"[ch // 2], (N_OUT + 1, N_OUT + 1, N_FFN2)[ch // 2])
                square(2, ch, ch % 2)
            ffn(1, N_FFN2, N_DOWN2)

            act.wait_ge(s_stat, 3)
            fn(sumsq[:], ps[:, B_ST, 0:NB], ACT.Ln, bias=eps[:, 0:1], scale=1.0 / D).then_inc(s_fl, 1)
            act.wait_ge(s_fl, 1)
            fn(sumsq[:], sumsq[:], ACT.Exp, scale=-0.5).then_inc(s_fr, 1)
            act.wait_ge(s_fr, 1)
            by_token_out(KC - 1, 1)
            act.wait_ge(s_fo, KC + 2)
            for b in range(2):
                fn(o_nat[:, b, :], o_nat[:, b, :], ACT.Copy, scale=sumsq[:, b:b + 1]).then_inc(s_fs[0], 1)

        @block.vector
        def _(dve):
            tt, stt = nc.vector.tensor_tensor, nc.vector.scalar_tensor_tensor

            def lo(name, n):
                s = slots[name]
                dve.wait_ge(s["his"], n + 1)
                tt(s["lo"], s["raw"], s["hi"].bitcast(f32), ALU.subtract).then_inc(s["split"], 1)

            for s in slots.values():
                dve.sem_inc(s["split"], 1)
            dve.sem_inc(s_xn, 2)
            dve.sem_inc(s_gu, 2)
            dve.sem_inc(s_wlo, 2)
            dve.sem_inc(s_ot, 1)
            dve.sem_inc(s_modv, 1)
            dve.wait_ge(s_vect, 1)
            nc.vector.tensor_copy(vecs[:], ps[:, 4, 0:120]).then_inc(s_vecs, 1)

            for b in range(NB):
                dve.wait_ge(s_sumsq, b + 1)
                if b >= 2:
                    dve.wait_ge(s_bcast, b - 1)
                nc.vector.tensor_scalar(diag[:, b % 2, :], ident[:], sumsq[:, b:b + 1], None, ALU.mult).then_inc(s_diag, 1)

            for ch in range(1, KC, 2):
                dve.wait_ge(s_xt, ch + 1)
                nc.vector.tensor_copy(X(ch), bank(1)).then_inc(s_xev[1], 1)
            dve.wait_ge(s_brow, 1)
            nc.vector.tensor_copy(brow[0:8, 0:512], ps[0:8, 2, :]).then_inc(s_browc, 1)
            nc.vector.tensor_copy(brow[0:8, 512:640], ps[0:8, 3, 0:128]).then_inc(s_browc, 1)

            def add_squares(k, ch, buf):
                dve.wait_ge(s_sq, KC * (k - 1) + ch + 1)
                dve.wait_ge(s_ssum, KC * (k - 1) + ch + 1)
                tt(ssum, ssum, gut[buf], ALU.add).then_inc(s_ssum, 1)

            def ada_first(n):
                dve.wait_ge(s_adav, n + 1)
                a = ada0[ADA_DVE[n]][:, :, :, :].rearrange("p t m n -> p t (m n)")
                tt(a[:, 0:4, :], a[:, 0:4, :], a[:, 4:8, :], ALU.add).then_inc(s_sumv, 1)
                dve.wait_ge(s_sumv, 2 * n + 1)
                tt(a[:, 0:2, :], a[:, 0:2, :], a[:, 2:4, :], ALU.add).then_inc(s_sumv, 1)

            def mod_first(ch):
                dve.wait_ge(s_mod0, ch + 1)
                tt(mod[:, ch:ch + KC + 1:KC], ps[:, B_MOD0[ch % 3], 0:2], vecs[:, ch:ch + KC + 1:KC], ALU.add).then_inc(s_modv0, 1)
                dve.wait_ge(s_modv0, ch + 1)
                stt(amp[:, ch:ch + 1], mod[:, KC + ch:KC + ch + 1], 1.0, vecs[:, 80 + ch:81 + ch], ALU.add, ALU.mult).then_inc(s_amp0, 1)
                dve.wait_ge(s_amp0, ch + 1)

            def ada_vec(n, col):
                dve.wait_ge(s_adam, n + 3)
                o = 2 * ADA_FIRST + 2 * n
                tt(mod[:, ds(o, 2)], ps[:, B_MOD, col:col + 2], vecs[:, ds(o, 2)], ALU.add).then_inc(s_modv, 1)

            def amplitude(k, count):
                stt(amp[:, KC * k:KC * k + KC], mod[:, 24 * k + 8:24 * k + 16], 1.0, vecs[:, 80 + 8 * k:88 + 8 * k],
                    ALU.add, ALU.mult).then_inc(s_amp, 1)
                dve.wait_ge(s_amp, count)

            def gate_of(k, factor, count):
                nc.vector.tensor_scalar(hgate[:, KC * k:KC * k + KC], mod[:, 24 * k + 16:24 * k + 24], factor, None,
                                        ALU.mult).then_inc(s_amp, 1)
                dve.wait_ge(s_amp, count)

            def modulated(k):
                dve.wait_ge(s_rstd, k + 1)

                def h_lo(ch):
                    dve.wait_ge(s_hh, KC * k + ch + 1)
                    stt(hl[:, ch, :], tmp[:, ch % 4, :], mod[:, 24 * k + ch:24 * k + ch + 1], hh[:, ch, :].bitcast(f32),
                        ALU.add, ALU.subtract).then_inc(s_hl, 1)

                for ch in range(KC):
                    if k == 0:
                        mod_first(ch)
                        dve.wait_ge(s_xev[ch % 2], ch // 2 + 1)
                    if ch >= 4:
                        dve.wait_ge(s_hl, KC * k + ch - 3)
                    stt(tmp[:, ch % 4, :], X(ch), amp[:, KC * k + ch:KC * k + ch + 1], ssum, ALU.mult, ALU.mult).then_inc(s_t, 1)
                    if k == 0:
                        if ch == 0:
                            lo("A", N_FFN1)
                        if ch in (1, 4):
                            ada_first(ch // 2)
                        h_lo(ch)
                        if ch == 0:
                            lo("B", N_FFN1)
                        if ch == 2:
                            ada_first(1)
                    elif ch >= 1:
                        h_lo(ch - 1)
                if k > 0:
                    h_lo(KC - 1)
                nc.vector.memset(ssum, 0.0).then_inc(s_ssum, 1)

            def residual(y, ch, b, buf, k, g, last):
                dve.wait_ge(s_y, y + 1)
                xs = xT[:, ds(ch * SEQ, SEQ)]
                stt(xs, bank(b), hgate[:, ds(ch + KC * g, 1)], xs, ALU.mult, ALU.add).then_inc(s_xn, 1)
                if not last:
                    add_squares(k, ch, buf)

            def ffn(f, n0, n1):
                modulated(2 * f)
                dve.wait_ge(s_browd, 16)

                def gate(i, with_ada):
                    j0 = 2 * i + FC * f
                    if with_ada:
                        ada_vec(2 * i - 2, 0)
                    lo("A", n0 + i + 1)
                    for r in range(2):
                        dve.wait_ge(s_sil, j0 + r + 3)
                        dve.wait_ge(s_up, j0 + r + 1)
                        tt(gut[r], sil[r], bank(2 + r), ALU.mult).then_inc(s_gu, 1)
                        dve.wait_ge(s_guh, j0 + r + 1)
                        o = i * 1024 + SEQ * r
                        tt(gul[:, ds(o, SEQ)], gut[r], guh[:, ds(o, SEQ)].bitcast(f32), ALU.subtract).then_inc(s_gul, 1)
                    lo("B", n0 + i + 1)
                    if with_ada:
                        ada_vec(2 * i - 1, 2)

                if f == 0:
                    gate(0, False)
                with dve.Fori(1 - f, GB) as i:
                    gate(i, f == 0)
                if f == 0:
                    dve.wait_ge(s_modv, D // ADA_COLS + 1)
                    gate_of(0, 0.5, 1)

                def down(m, r, last=False):
                    if not last:
                        lo("A", n1 + m + 1)
                    if f == 0:
                        ada_vec(m + ADA_DOWN, 2 * r)
                    residual(Y_FFN2 * f + m, m, B_Y[r], r, 2 * f + 1, 2 * f, last)
                    if f == 1:
                        dve.wait_ge(s_xn, Y_FFN2 + m + 3)
                        dve.wait_ge(s_ft, m + 1)
                        nc.vector.tensor_scalar(sil[r], xT[:, ds(m * SEQ, SEQ)], vecs[:, ds(m + 104, 1)], None,
                                                ALU.mult).then_inc(s_fy, 1)
                    if not last:
                        lo("B", n1 + m + 1)

                down(0, 0)
                with dve.Fori(0, DB // 2 - 1) as i:
                    for r in range(2):
                        down(2 * i + 1 + r, 1 - r)
                down(7, 1, last=True)

            ffn(0, N_FFN1, N_DOWN1)

            def q_lo(p):
                dve.wait_ge(s_qh, p + 1)
                for r, o in enumerate(own):
                    last = stt(ql[o, :], ps[o, B_P, :], DH ** -0.5, qs[r][o, :].bitcast(f32), ALU.mult, ALU.subtract)
                last.then_inc(s_qr, 1)

            def k_lo(p, first=False):
                dve.wait_ge(s_kh, p + 1)
                if not first:
                    dve.wait_ge(s_kd, 32 * p)
                for r, o in enumerate(own):
                    last = tt(kl[o, :], ps[o, B_O, :], ks[r][o, :].bitcast(f32), ALU.subtract)
                last.then_inc(s_kr, 1)

            def v_lo(p):
                dve.wait_ge(s_vh, p + 1)
                tt(vpl[:, :, 0:3:2, :], by_token, vph[:, :, 0:3:2, :].bitcast(f32), ALU.subtract).then_inc(s_vr, 1)

            def stick_abs(h, r):
                dve.wait_ge(s_s, h + 1)
                for e, z in two(E[r], B_Z[r]):
                    last = nc.vector.tensor_scalar(e.bitcast(i32), z.bitcast(i32), 0x7FFFFFFF, None, ALU.bitwise_and)
                last.then_inc(s_abs, 1)

            def stick_softplus(h, r):
                dve.wait_ge(s_l, h + 1)
                for e, z in two(E[r], B_Z[r]):
                    last = stt(e, z, 0.0, e, ALU.max, ALU.add)
                last.then_inc(s_sp, 1)

            def softplus_lo(h, r):
                dve.wait_ge(s_sph, h + 1)
                tt(ml[r][:], E[r][:], mh[r][:].bitcast(f32), ALU.subtract).then_inc(s_spl, 1)

            def stick_lo(h, r):
                dve.wait_ge(s_wh, h + 1)
                tt(ml[r][:], E[r][:], mh[r][:].bitcast(f32), ALU.subtract).then_inc(s_wlo, 1)

            def dil_scores(h, r):
                dve.wait_ge(s_s, h + 1)
                dve.wait_ge(s_tbl[r], 8 * (h - r) - 16 * N_SB + 16)
                nc.vector.memset(carrier[:], 0.0)
                for n in range(NB):
                    b, o = PB[n]
                    last = nc.vector.tensor_tensor_reduce(
                        out=part(E[r], n), in0=ps[:, B_Z[r] + b, o:o + WID[n]], in1=tbl[r][:, P * n:SEQ],
                        scale=1.0, scalar=-3.0e38, op0=ALU.add, op1=ALU.max, accum_out=stats[:, r, 0, n:n + 1])
                last.then_inc(s_zt, 1)
                dve.wait_ge(s_zt, h - H0 + 1)
                nc.vector.tensor_scalar(stats[:, r, 1, :], stats[:, r, 0, :], -1.0, None, ALU.mult).then_inc(s_nm, 1)

            def dil_normal(h, r):
                dve.wait_ge(s_ex, h - H0 + 1)
                nc.vector.reciprocal(stats[:, r, 3, :], stats[:, r, 2, :]).then_inc(s_rd, 1)
                dve.wait_ge(s_rd, h - H0 + 1)
                for n in range(NB):
                    last = nc.vector.tensor_scalar(part(E[r], n), part(E[r], n), stats[:, r, 3, n:n + 1], None, ALU.mult)
                last.then_inc(s_pn, 1)

            def dil_lo(h, r):
                dve.wait_ge(s_wh, h + 1)
                for (l, z), (w, _) in zip(two(ml[r], B_Z[r]), two(mh[r], B_Z[r])):
                    last = tt(l, z, w.bitcast(f32), ALU.subtract)
                last.then_inc(s_wlo, 1)

            def out_norm(p, b=B_O):
                dve.wait_ge(s_ors, p + 1)
                stt(sil[0], bank(b), vecs[:, ds(p + 112, 1)], sil[1], ALU.mult, ALU.mult).then_inc(s_ot, 1)

            def out_lo(p):
                dve.wait_ge(s_oh, p + 1)
                o = ds(p * SEQ, SEQ)
                tt(oTl[:, o], sil[0], oTh[:, o].bitcast(f32), ALU.subtract).then_inc(s_ol, 1)

            def mix_pair(p, dil, first=False, proj=True, more=True):
                h = 2 * p
                scores = dil_scores if dil else stick_abs
                scores(h, 0)
                if not first:
                    out_norm(p - 1)
                scores(h + 1, 1)
                if not first:
                    out_lo(p - 1)
                for r in range(2):
                    if dil:
                        dil_normal(h + r, r)
                    else:
                        stick_softplus(h + r, r)
                        softplus_lo(h + r, r)
                if proj:
                    q_lo(p + 1)
                    k_lo(p + 1)
                for r in range(2):
                    (dil_lo if dil else stick_lo)(h + r, r)
                if not more:
                    lo("A" if proj else "B", N_OUT)
                if proj:
                    v_lo(p + 1)

            dve.wait_ge(s_modv, ADA_LOOP + 1)
            amplitude(1, 2)
            gate_of(1, 1.0, 3)
            amplitude(2, 4)
            gate_of(2, 0.5, 5)
            modulated(1)
            q_lo(0)
            k_lo(0, first=True)
            v_lo(0)
            mix_pair(0, False, first=True)
            with dve.Fori(1, N_SB) as p:
                mix_pair(p, False)
            with dve.Fori(N_SB, PAIRS - 2) as p:
                mix_pair(p, True)
            mix_pair(PAIRS - 2, True, more=False)
            mix_pair(PAIRS - 1, True, proj=False, more=False)
            out_norm(PAIRS - 1, B_LAST)
            out_lo(PAIRS - 1)

            for ch in range(KC):
                residual(Y_OUT + ch, ch, B_OUT[ch], ch % 2, 2, 1, ch == KC - 1)
                if ch in (0, 2, 4):
                    lo("ABA"[ch // 2], (N_OUT + 1, N_OUT + 1, N_FFN2)[ch // 2])
            ffn(1, N_FFN2, N_DOWN2)

            dve.wait_ge(s_fr, 1)
            dve.wait_ge(s_fo, KC + 2)
            for b in range(2, NB):
                nc.vector.tensor_scalar(o_nat[:, b, :], o_nat[:, b, :], sumsq[:, b:b + 1], None, ALU.mult).then_inc(s_fs[1], 1)

        @block.tensor
        def _(pe):
            mm = nc.tensor.matmul

            def product(dst, w_h, w_l, a_h, a_l, start, stop):
                mm(dst, w_h, a_h, start=start, stop=False, skip_group_check=True)
                mm(dst, w_h, a_l, start=False, stop=False, skip_group_check=True)
                return mm(dst, w_l, a_h, start=False, stop=stop, skip_group_check=True)

            def tile(name, t, cols, col):
                s = slots[name]
                o = t * cols + col
                return s["hi"][:, o:o + P], s["lo"][:, o:o + P]

            pe.sem_inc(s_ft, 2)
            pe.sem_inc(s_adam, 2)

            pe.wait_ge(s_vec, 128)
            pe.wait_ge(s_ident, 1)
            nc.tensor.transpose(ps[:, 4, 0:120], rows[0:120, :], ident[0:120, 0:120]).then_inc(s_vect, 1)
            pe.wait_ge(s_ones, 1)
            for b in range(NB):
                pe.wait_ge(s_diag, b + 1)
                mm(ps[:, B_ST, P * b:P * b + P], ones[:], diag[:, b % 2, :], start=True, stop=True).then_inc(s_bcast, 1)
            pe.wait_ge(s_x, 16)
            for ch in range(KC):
                if ch >= 2:
                    pe.wait_ge(s_xev[ch % 2], ch // 2)
                for b in range(NB):
                    last = nc.tensor.transpose(ps[:, ch % 2, P * b:P * b + P], x_nat[:, b, P * ch:P * ch + P], ident[:])
                last.then_inc(s_xt, 1)
            pe.wait_ge(s_oneh, 32)
            mm(ps[0:8, 2, :], rel[0:33, 0:8], oneh[0:33, 0:512], start=True, stop=True)
            mm(ps[0:8, 3, 0:128], rel[0:33, 0:8], oneh[0:33, 512:640], start=True, stop=True).then_inc(s_brow, 1)

            def stat(k):
                pe.wait_ge(s_ssum, KC * k)
                mm(bank(B_ST), ones[:], ssum, start=True, stop=False, skip_group_check=True)
                pe.wait_ge(s_sq, KC * k)
                mm(bank(B_ST), ones[:], gut[1], start=False, stop=True, skip_group_check=True).then_inc(s_stat, 1)

            def modulation_first(ch):
                if ch in ADA_POOL:
                    pe.wait_ge(s_sump, ADA_POOL.index(ch) + 1)
                else:
                    pe.wait_ge(s_sumv, 2 * ADA_DVE.index(ch) + 2)
                if ch >= 3:
                    pe.wait_ge(s_modv0, ch - 2)
                for m in range(2):
                    for t in range(2):
                        last = mm(ps[:, B_MOD0[ch % 3], m:m + 1], ada0[ch][:, t, m, :], ones[:, 0:1], start=t == 0,
                                  stop=t == 1)
                last.then_inc(s_mod0, 1)

            def keep_clock(w, a, count):
                for _ in range(count):
                    mm(bank(B_Y[1]), w, a, start=True, stop=True)

            def ada_block(n, r, col):
                pe.wait_ge(s_adap, n + 2)
                pe.wait_ge(s_modv, n + 1)
                for e in range(2):
                    last = mm(ps[:, B_MOD, col + e:col + e + 1], ada_acc[:, r, P * e:P * e + P], ones[:, 0:1],
                              start=True, stop=True)
                last.then_inc(s_adam, 1)

            def by_token_out(ch, r):
                pe.wait_ge(s_fy, ch + 1)
                pe.wait_ge(s_fo, ch + 1)
                for b in range(NB):
                    last = nc.tensor.transpose(ps[:, r, P * b:P * b + P], sil[r][:, P * b:P * b + P], ident[:])
                last.then_inc(s_ft, 1)

            def ffn(f, n0, n1):
                early = range(3 - f)

                def first_product(b, k):
                    if b == 2 and k == 0:
                        pe.wait_ge(slots["B"]["split"], n0 + 2)
                    w_h, w_l = tile("AB"[b // 2], k, 256, P * (b % 2))
                    last = product(bank(b), w_h, w_l, hh[:, k, :], hl[:, k, :], k == 0, k == KC - 1)
                    if k == KC - 1:
                        last.then_inc(s_gate if b < 2 else s_up, 1)

                if f == 0:
                    modulation_first(0)
                    keep_clock(ones[:], x_nat[:, 0, 0:SEQ], 5)
                    modulation_first(1)
                pe.wait_ge(slots["A"]["split"], n0 + 2)
                if f == 1:
                    keep_clock(w_hi[:, 0:P], w_hi[:, 0:SEQ], 12)
                pe.wait_ge(s_sil, FC * f + 2)
                pe.wait_ge(s_gu, FC * f + 2)
                for k in range(KC):
                    if f == 0 and k == 0:
                        pe.wait_ge(s_browc, 2)
                    pe.wait_ge(s_hl, 16 * f + k + 1)
                    for b in early:
                        first_product(b, k)
                        if f == 0 and b == (2 if k == 0 else 1) and k + 2 < KC:
                            modulation_first(k + 2)
                for b in range(len(early), 4):
                    for k in range(KC):
                        first_product(b, k)
                if f == 0:
                    pe.wait_ge(s_modv0, KC)
                with pe.Fori(1, GB) as i:
                    j0 = 2 * i + FC * f
                    for name, free, done, b0 in (("A", s_sil, s_gate, 0), ("B", s_gu, s_up, 2)):
                        pe.wait_ge(slots[name]["split"], n0 + i + 2)
                        for r in range(2):
                            pe.wait_ge(free, j0 + r + 1)
                            for k in range(KC):
                                w_h, w_l = tile(name, k, 256, P * r)
                                last = product(bank(b0 + r), w_h, w_l, hh[:, k, :], hl[:, k, :], k == 0, k == KC - 1)
                            last.then_inc(done, 1)
                        if f == 0:
                            e = int(name == "B")
                            ada_block(2 * i - 2 + e, e, 2 * e)

                def down(m, r, first=False):
                    pe.wait_ge(s_xn, m + Y_FFN2 * f + 1)
                    for n, name in enumerate("AB"):
                        pe.wait_ge(slots[name]["split"], n1 + m + 2)
                        pe.wait_ge(s_gul, FC * f + 11 * n + 11)
                        for k in range(11):
                            w_h, w_l = tile(name, k, P, 0)
                            o = SEQ * (11 * n + k)
                            last = product(bank(B_Y[r]), w_h, w_l, guh[:, o:o + SEQ], gul[:, o:o + SEQ],
                                           n == 0 and k == 0, n == 1 and k == 10)
                        if n == 0:
                            last.then_inc(s_half, 1)
                            if f == 0:
                                ada_block(m + ADA_DOWN, r, 2 * r)
                            if f == 1 and not first:
                                by_token_out(m - 1, 1 - r)
                    last.then_inc(s_y, 1)

                down(0, 0, first=True)
                with pe.Fori(0, DB // 2 - 1) as i:
                    for r in range(2):
                        down(2 * i + 1 + r, 1 - r)
                down(7, 1)

            ffn(0, N_FFN1, N_DOWN1)
            stat(1)

            def project(name, p, b, free, count, done):
                pe.wait_ge(slots[name]["split"], p + 2)
                pe.wait_ge(free, count)
                for k in range(KC):
                    w_h, w_l = tile(name, k, P, 0)
                    last = product(bank(b), w_h, w_l, hh[:, k, :], hl[:, k, :], k == 0, k == KC - 1)
                last.then_inc(done, 1)

            def values_by_token(p):
                pe.wait_ge(s_vsb, p + 1)
                for b in range(NB):
                    last = nc.tensor.transpose(ps[:, B_P, P * b:P * b + P], vsb[:, P * b:P * b + P], ident[:])
                last.then_inc(s_vt, 1)

            def stick_scores(h, r):
                f = own[r]
                for j in range(NB):
                    b, o = PB[j]
                    dst = ps[:, B_Z[r] + b, o:o + WID[j]]
                    keys, queries = slice(P * j, P * j + P), slice(P * j, SEQ)
                    mm(dst, ks[r][:, keys], qs[r][:, queries], start=j < 3, stop=False, skip_group_check=True)
                    mm(dst, ks[r][f, keys], ql[f, queries], start=False, stop=False, skip_group_check=True)
                    last = mm(ps[:, B_Z[r] + b, o:o + P], ident_r, negm, start=False, stop=True, skip_group_check=True)
                last.then_inc(s_s, 1)

            def stick_suffix(h, r):
                pe.wait_ge(s_spl, h + 1)
                for j in range(NB):
                    b, o = PB[j]
                    for jj in range(j, NB):
                        dst = ps[:, B_Z[r] + b, o + P * (jj - j):o + WID[j]]
                        for t in (mh[r], ml[r]):
                            last = mm(dst, ntri if jj == j else nones, part(t, jj), start=False, stop=True,
                                      skip_group_check=True)
                last.then_inc(s_tr, 1)

            def dil_scores(h, r):
                f = own[r]
                for n in range(NB):
                    b, o = PB[n]
                    dst = ps[:, B_Z[r] + b, o:o + WID[n]]
                    i = NB - 1 - n
                    queries, keys = slice(P * i, P * i + P), slice(0, WID[n])
                    mm(dst, qs[r][:, queries], ks[r][:, keys], start=n < 3, stop=False, skip_group_check=True)
                    last = mm(dst, ql[f, queries], ks[r][f, keys], start=False, stop=True, skip_group_check=True)
                last.then_inc(s_s, 1)

            def dil_transpose(h, r):
                pe.wait_ge(s_pn, h - H0 + 1)
                for i in range(NB):
                    for j in range(i + 1):
                        b, o = PB[j]
                        src = E[r][:, OFF[NB - 1 - i] + P * j:OFF[NB - 1 - i] + P * j + P]
                        o += P * (i - j)
                        last = nc.tensor.transpose(ps[:, B_Z[r] + b, o:o + P], src, ident[:])
                last.then_inc(s_tr, 1)

            def attend(h, r, b=B_O):
                pe.wait_ge(s_wlo, h + 3)
                for j in range(NB):
                    v_h, v_l = (v[:, j].rearrange("p e n -> p (e n)")[:, DH * r:DH * r + P] for v in (vph, vpl))
                    last = product(ps[:, b, P * j:SEQ], v_h, v_l, part(mh[r], j), part(ml[r], j), r == 0 and j == 0,
                                   j == NB - 1)
                last.then_inc(s_avh, 1)

            def scores(p, r, dil):
                pe.wait_ge(s_qr, p + 1)
                pe.wait_ge(s_qd, 32 * p + 32)
                pe.wait_ge(s_kd, 32 * p + 32)
                pe.wait_ge(s_wlo, 2 * p + r + 1)
                (dil_scores if dil else stick_scores)(2 * p + r, r)

            def out_stat(p, b=B_P):
                pe.wait_ge(s_osq, p + 1)
                mm(bank(b), halves, gut[0], start=True, stop=True).then_inc(s_ost, 1)

            def mix_pair(p, dil, first=False):
                h = 2 * p
                transform = dil_transpose if dil else stick_suffix
                scores(p, 0, dil)
                pe.wait_ge(s_vr, p + 1)
                if not first:
                    out_stat(p - 1)
                scores(p, 1, dil)
                project("q", p + 1, B_P, s_oln, p + 1, s_pq)
                project("k", p + 1, B_O, s_ot, p + 1, s_pk)
                transform(h, 0)
                transform(h + 1, 1)
                project("v", p + 1, B_P, s_qr, p + 2, s_pv)
                pe.wait_ge(s_kr, p + 2)
                attend(h, 0)
                attend(h + 1, 1)
                values_by_token(p + 1)

            pe.wait_ge(slots["q"]["split"], 2)
            pe.wait_ge(slots["k"]["split"], 2)
            keep_clock(w_hi[:, 0:P], w_hi[:, 0:SEQ], 12)
            for k in range(KC):
                pe.wait_ge(s_hl, KC + k + 1)
                for name, b, done in (("q", B_P, s_pq), ("k", B_O, s_pk)):
                    w_h, w_l = tile(name, k, P, 0)
                    last = product(bank(b), w_h, w_l, hh[:, k, :], hl[:, k, :], k == 0, k == KC - 1)
                    if k == KC - 1:
                        last.then_inc(done, 1)
            project("v", 0, B_Z[0], s_stat, 1, s_pv)
            pe.wait_ge(s_kr, 1)
            pe.wait_ge(s_maskr, 1)
            values_by_token(0)
            mix_pair(0, False, first=True)
            with pe.Fori(1, N_SB) as p:
                mix_pair(p, False)
            with pe.Fori(N_SB, PAIRS - 2) as p:
                mix_pair(p, True)
            mix_pair(PAIRS - 2, True)

            def out_part(ch, pairs):
                name = "AABB"[ch % 4]
                pe.wait_ge(slots[name]["split"], N_OUT + ch // 4 + 2)
                for k in pairs:
                    pe.wait_ge(s_ol, k + 1)
                    w_h, w_l = tile(name, k, 256, P * (ch % 2))
                    o = SEQ * k
                    last = product(bank(B_OUT[ch]), w_h, w_l, oTh[:, o:o + SEQ], oTl[:, o:o + SEQ], k == 0, k == PAIRS - 1)
                if k == PAIRS - 1:
                    last.then_inc(s_y, 1)

            p, h = PAIRS - 1, 2 * PAIRS - 2
            scores(p, 0, True)
            pe.wait_ge(s_vr, p + 1)
            out_stat(p - 1)
            scores(p, 1, True)
            pe.wait_ge(s_oln, p + 1)
            out_part(0, range(0, 6))
            pe.wait_ge(s_ot, p + 1)
            out_part(1, range(0, 2))
            dil_transpose(h, 0)
            out_part(0, range(6, 7))
            out_part(1, range(2, 3))
            dil_transpose(h + 1, 1)
            out_part(1, range(3, 6))
            attend(h, 0, B_LAST)
            out_part(1, range(6, 7))
            attend(h + 1, 1, B_LAST)
            out_part(2, range(0, 4))
            out_stat(p, B_OUT[5])
            out_part(2, range(4, 7))
            out_part(3, range(0, 2))
            for ch in range(3):
                out_part(ch, range(7, 8))
            out_part(3, range(2, 8))
            for ch in range(4, KC):
                out_part(ch, range(8))
            stat(2)
            ffn(1, N_FFN2, N_DOWN2)

            for src in (ssum, gut[1]):
                if src is ssum:
                    pe.wait_ge(s_ssum, 3 * KC)
                else:
                    pe.wait_ge(s_sq, 3 * KC)
                for b in range(NB):
                    last = mm(ps[:, B_ST, b:b + 1], src[:, P * b:P * b + P], ones[:, 0:1],
                              start=src is ssum and b == 0, stop=src is not ssum, skip_group_check=True)
            last.then_inc(s_stat, 1)
            by_token_out(KC - 1, 1)


_INS = ["x", "c", "w_ada", "b_ada", "g_ffn1", "w1_gate", "w1_up", "w1_down", "g_mix", "w_in", "g_sb_out", "g_dil_out",
        "w_out", "rel_bias", "g_ffn2", "w2_gate", "w2_up", "w2_down", "g_final"]


def _shape_constants():
    import math
    k, q = np.arange(P)[:, None], np.arange(P)[None, :]
    masks = np.stack([
        (k == q).astype(np.float32),
        -(k >= q).astype(np.float32),
        -np.ones((P, P), np.float32),
        np.where(k < q, 0, NEG).astype(np.float32),
        (k // DH == q // DH).astype(np.float32),
    ])
    n = SEQ - 1 - np.arange(ROW)
    near = np.maximum(n, 0)
    large = 16 + (np.log(np.maximum(near, 1).astype(np.float32) / 16) / math.log(2048 / 16) * 16).astype(np.int32)
    bucket = np.where(near < 16, near, np.minimum(large, 31))
    times = (n <= 128).astype(int) + (n % 4 == 0) + (n % 16 == 0)
    times = np.where(n >= 0, times, 0)
    onehot = np.zeros((33, ROW), np.float32)
    onehot[bucket, np.arange(ROW)] = 1
    onehot[32] = np.where(times > 0, np.log(np.maximum(times, 1)), NEG)
    return masks, onehot


def kernel(**inputs):
    import concourse.bacc as bacc
    from concourse.bass_utils import run_bass_kernel_spmd

    nc = bacc.Bacc("TRN2", target_bir_lowering=False, num_devices=1)
    f32 = mybir.dt.float32
    arrays, args = {}, []
    feeds = [(name, np.ascontiguousarray(inputs[name])) for name in _INS]
    feeds += list(zip(("masks", "onehot"), _shape_constants()))
    for name, a in feeds:
        arrays[f"in_{name}"] = a
        args.append(nc.dram_tensor(f"in_{name}", a.shape, f32, kind="ExternalInput").ap())
    args.append(nc.dram_tensor("bias_rows", (8, ROW), f32, kind="Internal").ap())
    args.append(nc.dram_tensor("bias_copies", (8, P, ROW), f32, kind="Internal").ap())
    args.append(nc.dram_tensor("out_0", (1, SEQ, D), f32, kind="ExternalOutput").ap())
    build(nc, *args)
    r = run_bass_kernel_spmd(nc, [arrays], core_ids=[0])
    return r.results[0]["out_0"]
```
